# Optimizing a Trainium2 kernel written in Bass

```python
import jax, jax.numpy as jnp
from jax import lax
import numpy as np

D_MODEL = 2048
BATCH = 1
SEQ = 512
DEPTH = 1
DEC_BATCH = 8
DEC_SEQ = 1
PAST_LEN = 2048
PAGE_SIZE = 128

D_POOL = D_MODEL // 2
POOL_WINDOWS = (2, 4, 8, 16)
N_POOL_GROUPS = len(POOL_WINDOWS)
POOL_GROUP = D_POOL // N_POOL_GROUPS
POOL_MAX = max(POOL_WINDOWS)
D_ATTN = D_MODEL - D_POOL
HEAD_DIM = 64
N_HEADS = D_ATTN // HEAD_DIM
DILATED_PATTERNS = ((128, 1), (512, 4), (2048, 16))
WIN_MAX = max(w for w, _ in DILATED_PATTERNS)
BAND_BLOCK = 128
D_IN = 2 * D_POOL + 4 * D_ATTN
RMS_EPS = 1e-6

kernel_name = 'hybrid_pool_dilated_swa_step'

def rms_norm(x, g):
    xf = x.astype(jnp.float32)
    y = xf * lax.rsqrt(jnp.mean(xf * xf, axis=-1, keepdims=True) + RMS_EPS)
    return (y * g.astype(jnp.float32)).astype(x.dtype)

def alibi_slopes():
    return jnp.asarray(2.0 ** (-8.0 * np.arange(1, N_HEADS + 1) / N_HEADS), dtype=jnp.float32)

def split_proj(h, w_in):
    B, T, _ = h.shape
    z = jnp.einsum('btd,de->bte', h, w_in)
    cuts = [D_POOL, 2 * D_POOL, 2 * D_POOL + D_ATTN, 2 * D_POOL + 2 * D_ATTN, 2 * D_POOL + 3 * D_ATTN]
    u, gp, q, k, v, ga = jnp.split(z, cuts, axis=-1)
    heads = lambda a: a.reshape(B, T, N_HEADS, HEAD_DIM)
    return u, gp, heads(q), heads(k), heads(v), ga

def pool_mix(u, buf, pos0, w_lin, scale):
    B, T, _ = u.shape
    ext = jnp.concatenate([buf.astype(u.dtype), u], axis=1)
    cs = jnp.pad(jnp.cumsum(ext.astype(jnp.float32), axis=1), ((0, 0), (1, 0), (0, 0)))
    hi = cs[:, POOL_MAX:]
    pos = pos0 + jnp.arange(T)
    means = []
    for g, w in enumerate(POOL_WINDOWS):
        sl = slice(g * POOL_GROUP, (g + 1) * POOL_GROUP)
        lo = cs[:, POOL_MAX - w:POOL_MAX - w + T, sl]
        cnt = jnp.minimum(w, pos + 1).astype(jnp.float32)[None, :, None]
        means.append((hi[..., sl] - lo) / cnt)
    pooled = jnp.concatenate(means, axis=-1) - u.astype(jnp.float32)
    pooled = pooled.reshape(B, T, N_POOL_GROUPS, POOL_GROUP)
    mixed = jnp.einsum('btgc,gcd->btgd', pooled, w_lin.astype(jnp.float32)).reshape(B, T, D_POOL)
    mixed = mixed * scale.astype(jnp.float32)
    return mixed, ext[:, -(POOL_MAX - 1):]

def combine_patterns(outs, lses):
    w = jax.nn.softmax(jnp.stack(lses, axis=0), axis=0)
    return jnp.sum(w[..., None] * jnp.stack(outs, axis=0), axis=0)

def dilated_attn_prompt(q, k, v, slopes):
    B, T, H, E = q.shape
    scale = HEAD_DIM ** -0.5
    outs, lses = [], []
    for window, d in DILATED_PATTERNS:
        n_steps = window // d
        n_sub = T // d
        nb = -(-n_sub // BAND_BLOCK)
        n_pad = nb * BAND_BLOCK

        def to_blocks(a):
            a = a.reshape(B, n_sub, d, H, E).transpose(0, 2, 1, 3, 4)
            a = jnp.pad(a.astype(jnp.float32), ((0, 0), (0, 0), (0, n_pad - n_sub), (0, 0), (0, 0)))
            return a.reshape(B, d, nb, BAND_BLOCK, H, E)

        qb, kb, vb = to_blocks(q), to_blocks(k), to_blocks(v)
        prev = lambda a: jnp.concatenate([jnp.zeros_like(a[:, :, :1]), a[:, :, :-1]], axis=2)
        kk = jnp.concatenate([prev(kb), kb], axis=3)
        vv = jnp.concatenate([prev(vb), vb], axis=3)
        s = jnp.einsum('brnqhe,brnkhe->brnhqk', qb, kk) * scale
        qi = jnp.arange(BAND_BLOCK)[:, None] + BAND_BLOCK
        kj = jnp.arange(2 * BAND_BLOCK)[None, :]
        dist = qi - kj
        key_sub = jnp.arange(nb)[:, None, None] * BAND_BLOCK - BAND_BLOCK + kj[None]
        valid = (dist >= 0) & (dist <= n_steps) & (key_sub >= 0)
        bias = -slopes[:, None, None] * (dist * d).astype(jnp.float32)
        s = jnp.where(valid[:, None], s + bias[None], -jnp.inf)
        m = jnp.max(s, axis=-1, keepdims=True)
        p = jnp.exp(s - m)
        den = jnp.sum(p, axis=-1)
        den_t = den.transpose(0, 1, 2, 4, 3)
        o = jnp.einsum('brnhqk,brnkhe->brnqhe', p, vv) / den_t[..., None]
        lse = m[..., 0].transpose(0, 1, 2, 4, 3) + jnp.log(den_t)

        def from_blocks(a):
            a = a.reshape(B, d, n_pad, *a.shape[4:])[:, :, :n_sub]
            a = jnp.moveaxis(a, 1, 2)
            return a.reshape(B, T, *a.shape[3:])

        outs.append(from_blocks(o))
        lses.append(from_blocks(lse))
    return combine_patterns(outs, lses)

def dilated_attn_sample(q, k, v, k_buf, v_buf, slopes):
    L = k_buf.shape[1]
    S = q.shape[1]
    scale = HEAD_DIM ** -0.5
    k_all = jnp.concatenate([k_buf.astype(jnp.float32), k.astype(jnp.float32)], axis=1)
    v_all = jnp.concatenate([v_buf.astype(jnp.float32), v.astype(jnp.float32)], axis=1)
    qf = q.astype(jnp.float32)
    c = L + jnp.arange(S)
    outs, lses = [], []
    for window, d in DILATED_PATTERNS:
        steps = jnp.arange(window // d + 1)
        idx = c[:, None] - steps[None, :] * d
        valid = idx >= 0
        idx = jnp.maximum(idx, 0)
        kg = k_all[:, idx]
        vg = v_all[:, idx]
        s = jnp.einsum('bshe,bsnhe->bhsn', qf, kg) * scale
        bias = -slopes[:, None, None] * (steps * d).astype(jnp.float32)[None, None, :]
        s = jnp.where(valid[None, None], s + bias, -jnp.inf)
        m = jnp.max(s, axis=-1, keepdims=True)
        p = jnp.exp(s - m)
        den = jnp.sum(p, axis=-1)
        den_t = den.transpose(0, 2, 1)
        o = jnp.einsum('bhsn,bsnhe->bshe', p, vg) / den_t[..., None]
        lse = m[..., 0].transpose(0, 2, 1) + jnp.log(den_t)
        outs.append(o)
        lses.append(lse)
    return combine_patterns(outs, lses)

def merge_out(pm, gp, a, ga, w_out, dtype):
    B, T, _ = pm.shape
    f32 = jnp.float32
    mix = jnp.concatenate([pm * jax.nn.silu(gp.astype(f32)),
                           a.reshape(B, T, D_ATTN) * jax.nn.silu(ga.astype(f32))], axis=-1).astype(dtype)
    return jnp.einsum('btm,md->btd', mix, w_out)

def setup_inputs(seed: int = 0) -> dict:
    key = jax.random.key(seed)
    ks = jax.random.split(key, 12)
    l_win = min(WIN_MAX, PAST_LEN)
    f32 = jnp.float32
    return {
        'x_prompt': jax.random.normal(ks[0], (BATCH, SEQ, D_MODEL), f32),
        'x_sample': jax.random.normal(ks[1], (DEC_BATCH, DEC_SEQ, D_MODEL), f32),
        'state_pool': jax.random.normal(ks[2], (DEPTH, DEC_BATCH, POOL_MAX - 1, D_POOL), f32),
        'cache_k_win': jax.random.normal(ks[3], (DEPTH, DEC_BATCH, l_win, N_HEADS, HEAD_DIM), f32),
        'cache_v_win': jax.random.normal(ks[4], (DEPTH, DEC_BATCH, l_win, N_HEADS, HEAD_DIM), f32),
        'norm_g': 1.0 + 0.05 * jax.random.normal(ks[5], (DEPTH, D_MODEL), f32),
        'w_in': jax.random.normal(ks[6], (DEPTH, D_MODEL, D_IN), f32) * D_MODEL ** -0.5,
        'pool_w': jax.random.normal(ks[7], (DEPTH, N_POOL_GROUPS, POOL_GROUP, POOL_GROUP), f32) * POOL_GROUP ** -0.5,
        'pool_scale': 1.0 + 0.1 * jax.random.normal(ks[8], (DEPTH, D_POOL), f32),
        'w_out': jax.random.normal(ks[9], (DEPTH, D_POOL + D_ATTN, D_MODEL), f32) * (D_POOL + D_ATTN) ** -0.5,
        'final_norm_g': 1.0 + 0.05 * jax.random.normal(ks[10], (D_MODEL,), f32),
    }

def reference(x_prompt, x_sample, state_pool, cache_k_win, cache_v_win,
              norm_g, w_in, pool_w, pool_scale, w_out, final_norm_g):
    slopes = alibi_slopes()

    B, T, _ = x_prompt.shape
    keep = min(WIN_MAX, T)
    xp = x_prompt
    pool_p, k_p, v_p = [], [], []
    for l in range(DEPTH):
        h = rms_norm(xp, norm_g[l])
        u, gp, q, k, v, ga = split_proj(h, w_in[l])
        zero_buf = jnp.zeros((B, POOL_MAX - 1, D_POOL), u.dtype)
        pm, pbuf = pool_mix(u, zero_buf, 0, pool_w[l], pool_scale[l])
        a = dilated_attn_prompt(q, k, v, slopes)
        xp = xp + merge_out(pm, gp, a, ga, w_out[l], xp.dtype)
        pool_p.append(pbuf)
        k_p.append(k[:, T - keep:])
        v_p.append(v[:, T - keep:])
    y_prompt = rms_norm(xp, final_norm_g)

    xs = x_sample
    pool_s, k_s, v_s = [], [], []
    for l in range(DEPTH):
        h = rms_norm(xs, norm_g[l])
        u, gp, q, k, v, ga = split_proj(h, w_in[l])
        pm, pbuf = pool_mix(u, state_pool[l], PAST_LEN, pool_w[l], pool_scale[l])
        a = dilated_attn_sample(q, k, v, cache_k_win[l], cache_v_win[l], slopes)
        xs = xs + merge_out(pm, gp, a, ga, w_out[l], xs.dtype)
        pool_s.append(pbuf)
        k_s.append(k)
        v_s.append(v)
    y_sample = rms_norm(xs, final_norm_g)

    return (y_prompt, y_sample,
            jnp.stack(pool_p), jnp.stack(k_p), jnp.stack(v_p),
            jnp.stack(pool_s), jnp.stack(k_s), jnp.stack(v_s))


_drawn_inputs = setup_inputs


def setup_inputs(seed=0):
    import zlib

    import numpy as np

    out = dict(_drawn_inputs(seed))
    spreads = {}
    factors = {}
    for name, (base, spread) in spreads.items():
        noise = np.random.default_rng([zlib.crc32(name.encode()), seed]).standard_normal(out[name].shape)
        drawn = base * np.exp(spread * noise) if base else spread * noise
        out[name] = __import__('jax').numpy.asarray(drawn.astype(out[name].dtype))
    for name, factor in factors.items():
        out[name] = (out[name] * factor).astype(out[name].dtype)
    return out
```

```python
from contextlib import ExitStack

import concourse.bass as bass
import numpy as np
from concourse import mybir
from concourse.alu_op_type import AluOpType as ALU

F32 = mybir.dt.float32
F32R = mybir.dt.float32r
ACT = mybir.ActivationFunctionType
AX_X = mybir.AxisListType.X

P = 128
D_MODEL = 2048
SEQ = 512
NB = 8
NT = SEQ + NB
HT = NT // 2
D_HALF = 1024
HEADS, E = 16, 64
PAIRS = HEADS // 2
GROUPS = 4
WINDOWS = (2, 4, 8, 16)
PAST = 2048
HIST = 15
KT = D_MODEL // P
CHUNKS = ((0, 6), (6, 11), (11, 16))
CK = 6
SLOTS = 3
NCH = 18
COL_OF = (2048, 3072, 4096, 0, 1024, 5120)
TPB = 14
QT = SEQ // P
ROWS_T = (128, 97, 96)
LW = 16 + SEQ + 16 * NB
SCALE = float(E) ** -0.5
EPS = 1e-6
MASKED = 1e30

UNITS = (((0, 0), (1, 128)), ((2, 0),), ((3, 0),))

C_ID, C_DIST, C_NLOG, C_SLOPE, C_SB, C_INV, C_IW, C_LM, C_END = np.cumsum(
    [0, 128, 512, 512, 16, 48, 64, 4, 12]).tolist()


def constants():
    t = np.zeros((P, C_END), np.float32)
    t[:, C_ID:C_ID + P] = np.eye(P, dtype=np.float32)

    def count(d):
        return ((d >= 0) & (d <= 128)) * 1 + ((d >= 0) & (d <= 512) & (d % 4 == 0)) * 1 + \
            ((d >= 0) & (d <= 2048) & (d % 16 == 0)) * 1

    def neg_log(c):
        return np.where(c > 0, -np.log(np.maximum(c, 1)), MASKED)

    d = np.arange(P)[:, None] + 384 - np.arange(SEQ)[None, :]
    c = count(d)
    t[:, C_DIST:C_DIST + SEQ] = np.where(c > 0, d, 0)
    t[:, C_NLOG:C_NLOG + SEQ] = neg_log(c)
    slopes = (2.0 ** (-8.0 * np.arange(1, HEADS + 1) / HEADS)).astype(np.float32)
    t[:, C_SLOPE:C_SLOPE + HEADS] = slopes
    p = np.arange(P)
    ds = np.stack([128 - p, 512 - 4 * p, 2048 - 16 * p], 1)
    ds[96, 1] = 0
    live = np.stack([p < r for r in ROWS_T], 1)
    cs = np.where(live, count(ds), 0)
    sb = np.where(live, ds, 0)[:, :, None].astype(np.float32) * slopes + neg_log(cs)[:, :, None]
    t[:, C_SB:C_SB + 48] = sb.reshape(P, 48)
    for g, w in enumerate(WINDOWS):
        t[:, C_INV + 16 * g:C_INV + 16 * g + 16] = 1.0 / np.minimum(w, np.arange(16) + 1)
        t[:, C_IW + g] = 1.0 / w
        for j in range(3):
            t[:, C_LM + 3 * g + j] = 1.0 if j + 1 <= g else 0.0
    return t


def layer_step(nc, x_prompt, x_sample, state_pool, cache_k, cache_v, norm_g, w_in, pool_w,
               pool_scale, w_out, final_g, consts, y_prompt, y_sample, pool_state_p, k_win_p,
               v_win_p, pool_state_s, k_new, v_new):
    with ExitStack() as ctx:
        def sb(name, shape, dt=F32):
            return ctx.enter_context(nc.sbuf_tensor(name, shape, dt))

        def bank(name):
            return ctx.enter_context(nc.psum_tensor(name, [P, 512], F32))

        def sem(name):
            return ctx.enter_context(nc.semaphore(name))

        xp = x_prompt.rearrange("b (t p) d -> (b p) t d", p=P)
        xs = x_sample.rearrange("b s d -> (b s) d")
        wi = w_in.rearrange("l (k p) e -> (l p) k e", p=P)
        wo = w_out.rearrange("l (k p) e -> (l p) k e", p=P)
        pw = pool_w.rearrange("l g (c p) d -> (l g) p c d", p=P)

        def cache_rows(c):
            rows = c.rearrange("l b r h e -> (l b) r (h e)")

            def every(lo, hi, step):
                return rows[:, lo:hi, :].rearrange("b (r s) x -> r s b x", s=step)[:, 0]
            return every(1920, 2048, 1), every(1536, 1920, 4), every(0, 1536, 16)
        k_rows, v_rows = cache_rows(cache_k), cache_rows(cache_v)
        st = state_pool.rearrange("l b s c -> (l b s) c")
        k_out = k_win_p.rearrange("l b (t p) h e -> (l b p) t (h e)", p=P)
        v_out = v_win_p.rearrange("l b (t p) h e -> (l b p) t (h e)", p=P)
        kn_out = k_new.rearrange("l b s h e -> (l b s) (h e)")
        vn_out = v_new.rearrange("l b s h e -> (l b s) (h e)")
        psp_out = pool_state_p.rearrange("l b s c -> (l b s) c")
        pss_out = pool_state_s.rearrange("l b s c -> (l b) s c")
        pss_in = state_pool.rearrange("l b s c -> (l b) s c")
        yp = y_prompt.rearrange("b (t p) d -> (b p) t d", p=P)
        ys_out = y_sample.rearrange("b s d -> (b s) d")
        mix_dram = nc.dram_tensor("mix_scratch", [KT, P, NT], F32, kind="Internal").ap()
        row_dram = nc.dram_tensor("row_scratch", [3, NB, P], F32, kind="Internal").ap()

        mov_hi = sb("mov_hi", [P, KT, NT], F32R)
        mov_lo = sb("mov_lo", [P, KT, NT], F32R)
        w_hi = sb("w_hi", [P, SLOTS, CK, P], F32R)
        w_lo = sb("w_lo", [P, SLOTS, CK, P], F32R)
        q_hl = sb("q_hl", [P, SEQ], F32R)
        k_hh = sb("k_hh", [P, SEQ], F32R)
        k_ll = sb("k_ll", [P, SEQ], F32R)
        pt_hi = sb("pt_hi", [P, QT, SEQ], F32R)
        pt_lo = sb("pt_lo", [P, QT, SEQ], F32R)
        v_hl = sb("v_hl", [P, QT, 4 * E], F32R)
        pooled_hi = sb("pooled_hi", [P, 2, NT], F32R)
        pooled_lo = sb("pooled_lo", [P, 2, NT], F32R)
        pw_hi = sb("pw_hi", [P, 2, 256], F32R)
        pw_lo = sb("pw_lo", [P, 2, 256], F32R)
        av_hi = sb("av_hi", [P, NB * P], F32R)
        av_lo = sb("av_lo", [P, NB * P], F32R)
        ones_r = sb("ones_r", [P, P], F32R)

        w_raw = sb("w_raw", [P, SLOTS, CK, P])
        tab = sb("tab", [P, C_END])
        rstd_bc = sb("rstd_bc", [P, NT])
        stat = sb("stat", [P, 40])
        pscale = sb("pscale", [P, PAIRS])
        arena = sb("arena", [P, 15856])

        ident = tab[:, C_ID:C_ID + P]

        def carver():
            at = [0]

            def take(n):
                at[0] += n
                assert at[0] <= 15856, at[0]
                return arena[:, at[0] - n:at[0]]
            return take
        take = carver()
        x_nat = [take(D_MODEL) for _ in range(QT + 1)]
        g_bc = take(D_MODEL)
        junk = take(D_MODEL)
        diag = take(NT)
        ones_f = take(P)
        take = carver()
        z_q, z_k, z_v = take(NT), take(NT), take(NT)
        pbuf = [take(SEQ), take(SEQ)]
        z_gp = [take(NT), take(NT)]
        z_ga = take(NT)
        lev = [take(LW) for _ in range(3)]
        pooled = take(NT)
        k_nat, v_nat = take(SEQ), take(SEQ)
        nbias = take(SEQ)
        o_side = take(SEQ)
        attn = take(NT)
        th = take(NT)
        kv = take(3 * NB * P).rearrange("p (t x) -> p t x", t=3)
        q_bc = take(NB * P)
        rows = take(3 * P).rearrange("p (a x) -> p a x", a=3)
        pw_raw = take(512).rearrange("p (c d) -> p c d", c=2)
        st_nat = take(P)
        sc_s = take(48)
        ns_s = take(48)
        p_s = take(3 * P)
        pt_s = take(48)
        t16 = take(16)
        u_rows = take(2 * P).rearrange("p (a x) -> p a x", a=2)
        take = carver()
        mix_in = [take(NT) for _ in range(3)]
        y = take(QT * D_MODEL).rearrange("p (t d) -> p t d", t=QT)
        y_s = take(D_MODEL)
        y_t = [take(NT), take(NT)]
        x_res = [take(SEQ + P) for _ in range(2)]
        ss_y = take(5 * KT).rearrange("p (t d) -> p t d", t=5)
        sq_junk = take(P)
        gf_bc = w_raw[:, :, :, :].rearrange("p s k n -> p (s k n)")[:, 0:D_MODEL]

        ss, ms, sd, rstd = stat[:, 0:5], stat[:, 5:10], stat[:, 10:15], stat[:, 15:20]
        nmax, den, rden = stat[:, 20:24], stat[:, 24:28], stat[:, 28:32]
        nmax_s, den_s, rden_s = stat[0:16, 32:33], stat[0:16, 33:34], stat[0:16, 34:35]

        pj = [[bank(f"pj{a}{b}") for b in range(2)] for a in range(2)]
        ps_s = bank("ps_s")
        ps_t = bank("ps_t")
        ps_o = bank("ps_o")
        ps_m = bank("ps_m")

        x_in = [sem(f"x_in{i}") for i in range(QT + 1)]
        g_in, tab_in, ps_in, gf_in = sem("g_in"), sem("tab_in"), sem("ps_in"), sem("gf_in")
        squared = sem("squared")
        scaled = sem("scaled")
        x_turned = sem("x_turned")
        x_hi_done = sem("x_hi_done")
        x_lo_done = sem("x_lo_done")
        ms_done, sd_done, rs_done, diag_done, rb_done = (
            sem("ms_done"), sem("sd_done"), sem("rs_done"), sem("diag_done"), sem("rb_done"))
        cleared = sem("cleared")
        raw_in = [sem(f"raw_in{i}") for i in range(SLOTS)]
        w_hi_done = sem("w_hi_done")
        w_lo_done = sem("w_lo_done")
        w_used = sem("w_used")
        tile_done = sem("tile_done")
        tile_out = sem("tile_out")
        qk_hi_done = sem("qk_hi_done")
        qk_split = sem("qk_split")
        qk_rows_t, qk_rows_c = sem("qk_rows_t"), sem("qk_rows_c")
        v_rows_t, v_rows_c = sem("v_rows_t"), sem("v_rows_c")
        k_nat_t, k_nat_c = sem("k_nat_t"), sem("k_nat_c")
        v_nat_t, v_nat_c = sem("v_nat_t"), sem("v_nat_c")
        v_hi_done, v_split = sem("v_hi_done"), sem("v_split")
        bias_done = sem("bias_done")
        scores = sem("scores")
        biased = sem("biased")
        exped = sem("exped")
        recip = sem("recip")
        normed = sem("normed")
        p_turned = sem("p_turned")
        pt_hi_done = sem("pt_hi_done")
        pt_split = sem("pt_split")
        pv_done = sem("pv_done")
        side_done = sem("side_done")
        o_done = sem("o_done")
        st_in, st_t, st_c = sem("st_in"), sem("st_t"), sem("st_c")
        lev_done = sem("lev_done")
        mean_done = sem("mean_done")
        pooled_hi_done, pooled_split = sem("pooled_hi_done"), sem("pooled_split")
        u_rows_t, u_rows_c = sem("u_rows_t"), sem("u_rows_c")
        pw_in, pw_hi_done, pw_split = sem("pw_in"), sem("pw_hi_done"), sem("pw_split")
        gp_tanh, gp_gate = sem("gp_tanh"), sem("gp_gate")
        ga_tanh, ga_gate = sem("ga_tanh"), sem("ga_gate")
        row_wr = sem("row_wr")
        vrow_wr = sem("vrow_wr")
        q_bc_in, kn_in, vn_in = sem("q_bc_in"), sem("kn_in"), sem("vn_in")
        k_in, v_in = sem("k_in"), sem("v_in")
        kq_done = sem("kq_done")
        kq_sum = sem("kq_sum")
        ns_done, ns_t, mx_s, ex_s, rc_s, nr_s, pt_s_t, pt_s_c = (
            sem("ns_done"), sem("ns_t"), sem("mx_s"), sem("ex_s"), sem("rc_s"), sem("nr_s"),
            sem("pt_s_t"), sem("pt_s_c"))
        pv_s = sem("pv_s")
        av_add = sem("av_add")
        av_hi_done, av_split = sem("av_hi_done"), sem("av_split")
        av_sum = sem("av_sum")
        pick = sem("pick")
        mixed = sem("mixed")
        pool_mixed = sem("pool_mixed")
        mix_st, pmix_st = sem("mix_st"), sem("pmix_st")
        kn_st, vn_st, us_st, up_st = sem("kn_st"), sem("vn_st"), sem("us_st"), sem("up_st")
        kv_st, hist_st = sem("kv_st"), sem("hist_st")
        mix_back = [sem(f"mix_back{i}") for i in range(3)]
        m_hi_done, m_split = sem("m_hi_done"), sem("m_split")
        yt_done, y_turned, y_added, y_sq = sem("yt_done"), sem("y_turned"), sem("y_added"), sem("y_sq")
        xr_in = [sem("xr_in0"), sem("xr_in1")]
        xrs_in = [sem("xrs_in0"), sem("xrs_in1")]
        f_sum, f_ms, f_sd, f_rs, f_out, f_st = (
            sem("f_sum"), sem("f_ms"), sem("f_sd"), sem("f_rs"), sem("f_out"), sem("f_st"))
        unit_starts, rows_seen, stores_seen = (
            sem("unit_starts"), sem("rows_seen"), sem("stores_seen"))
        IN_TILES = TPB * GROUPS
        IN_CHUNKS = NCH * PAIRS

        block = ctx.enter_context(nc.Block())

        @block.sync
        def _(sp):
            sp.dma_start(x_nat[0], xp[:, 0, :]).then_inc(x_in[0], 16)
            sp.dma_start(g_bc, norm_g[0].partition_broadcast(P)).then_inc(g_in, 16)
            sp.dma_start(tab[:, :], consts).then_inc(tab_in, 16)
            for t in range(1, QT):
                sp.dma_start(x_nat[t], xp[:, t, :]).then_inc(x_in[t], 16)
            sp.dma_start(x_nat[QT][0:NB, :], xs).then_inc(x_in[QT], 16)
            with nc.allow_non_contiguous_dma(reason="1024 scales, once"):
                sp.dma_start(pscale[:, :], pool_scale[0].rearrange("(i p) -> p i", p=P)).then_inc(ps_in, 16)
            sp.dma_start(pss_out[:, 0:HIST - 1, :], pss_in[:, 1:HIST, :]).then_inc(hist_st, 16)

            def load_chunk(n, slot, src):
                sp.wait_ge(w_lo_done, n + 1)
                lo, hi = CHUNKS[slot]
                sp.dma_start(w_raw[:, slot, 0:hi - lo, :], src).then_inc(raw_in[slot], 16)

            with sp.Fori(0, GROUPS) as g:
                for half in range(2):
                    pr = 2 * g + half
                    for j in range(NCH):
                        lo, hi = CHUNKS[j % 3]
                        load_chunk(NCH * pr + j, j % 3,
                                   wi[:, lo:hi, bass.ds(COL_OF[j // 3] + P * pr, P)])
                        if j == 5:
                            sp.dma_start(st_nat[0:NB * HIST, :],
                                         st[:, bass.ds(P * pr, P)]).then_inc(st_in, 16)
                            for t, r in enumerate((128, 96, 96)):
                                sp.dma_start(kv[0:r, t, :].rearrange("p (b x) -> p b x", b=NB),
                                             k_rows[t][:, :, bass.ds(P * pr, P)]).then_inc(k_in, 16)
                            if half == 1:
                                sp.dma_start(pw_raw, pw[bass.ds(g, 1)].rearrange(
                                    "a p c d -> (a p) c d")).then_inc(pw_in, 16)
                        if j == 13:
                            sp.wait_ge(k_nat_c, pr + 1)
                            sp.dma_start(k_out[:, :, bass.ds(P * pr, P)],
                                         k_nat.rearrange("p (t x) -> p t x", t=QT)).then_inc(kv_st, 16)
                            sp.wait_ge(kq_sum, 3 * pr + 3)
                            for t, r in enumerate((128, 96, 96)):
                                sp.dma_start(kv[0:r, t, :].rearrange("p (b x) -> p b x", b=NB),
                                             v_rows[t][:, :, bass.ds(P * pr, P)]).then_inc(v_in, 16)
                        if j == 16:
                            sp.wait_ge(v_nat_c, pr + 1)
                            sp.dma_start(v_out[:, :, bass.ds(P * pr, P)],
                                         v_nat.rearrange("p (t x) -> p t x", t=QT)).then_inc(kv_st, 16)
                        if j == 17:
                            sp.wait_ge(kv_st, 32 * pr + 32)
                            sp.sem_inc(stores_seen, 1)

            for c in range(3):
                load_chunk(IN_CHUNKS + c, c, wo[:, CHUNKS[c][0]:CHUNKS[c][1], 0:P])
            sp.wait_ge(v_rows_t, PAIRS)
            sp.wait_ge(qk_split, 2 * PAIRS)
            sp.wait_ge(v_nat_t, PAIRS)
            for k in range(KT):
                if k < PAIRS:
                    sp.wait_ge(pmix_st, 16 * (k // 2 * 2 + 2))
                else:
                    sp.wait_ge(mix_st, 16 * (k - PAIRS + 1))
                if k >= 3:
                    sp.wait_ge(m_split, k - 2)
                sp.dma_start(mix_in[k % 3], mix_dram[k]).then_inc(mix_back[k % 3], 16)

            def load_res(d, q):
                sp.dma_start(x_res[q][:, 0:SEQ].rearrange("p (t x) -> p t x", t=QT),
                             xp[:, :, bass.ds(P * d, P)]).then_inc(xr_in[q], 16)
                sp.dma_start(x_res[q][0:NB, SEQ:SEQ + P],
                             xs[:, bass.ds(P * d, P)]).then_inc(xrs_in[q], 16)
            load_res(0, 0)
            load_res(1, 1)
            for c in range(3):
                load_chunk(IN_CHUNKS + 3 + c, c, wo[:, CHUNKS[c][0]:CHUNKS[c][1], P:2 * P])
            with sp.Fori(0, KT // 2 - 1) as i:
                for q in range(2):
                    for c in range(3):
                        lo, hi = CHUNKS[c]
                        load_chunk(IN_CHUNKS + 3 * (2 * i + q + 2) + c, c,
                                   wo[:, lo:hi, bass.ds(P * (2 * i + q + 2), P)])
                    sp.wait_ge(y_added, 2 * i + q + 1)
                    load_res(2 * i + q + 2, q)
            sp.wait_ge(w_lo_done, IN_CHUNKS + 3 * KT + 3)
            sp.dma_start(gf_bc, final_g.partition_broadcast(P)).then_inc(gf_in, 16)
            for t in range(QT):
                sp.wait_ge(f_out, t + 1)
                sp.dma_start(yp[:, t, :], y[:, t, :]).then_inc(f_st, 16)
            sp.wait_ge(f_out, QT + 1)
            sp.dma_start(ys_out, y_s[0:NB, :]).then_inc(f_st, 16)
            sp.wait_ge(f_st, 16 * (QT + 1))
            for s, n in ((kv_st, 2 * PAIRS), (kn_st, PAIRS), (vn_st, PAIRS),
                         (us_st, PAIRS), (up_st, PAIRS), (hist_st, 1), (mix_st, PAIRS),
                         (pmix_st, PAIRS), (row_wr, PAIRS), (vrow_wr, PAIRS)):
                sp.wait_ge(s, 16 * n)

        @block.tensor
        def _(pe):
            banks = [pj[0][0], pj[0][1], pj[1][0], pj[1][1]]
            pe.wait_ge(tab_in, 16)
            for t in range(QT):
                pe.wait_ge(scaled, t + 1)
                for kq in range(4):
                    u = 4 * t + kq
                    if u >= 4:
                        pe.wait_ge(x_lo_done, u - 3)
                    for i in range(4):
                        k = 4 * kq + i
                        last = pe.transpose(banks[u % 4][:, P * i:P * i + P],
                                            x_nat[t][:, P * k:P * k + P], ident)
                    last.then_inc(x_turned, 1)
            pe.wait_ge(scaled, QT + 1)
            pe.wait_ge(x_lo_done, 13)
            for k in range(KT):
                last = pe.transpose(banks[0][:, NB * k:NB * k + NB],
                                    x_nat[QT][0:NB, P * k:P * k + P], ident[0:NB, 0:NB])
            last.then_inc(x_turned, 1)
            pe.wait_ge(diag_done, 5)
            pe.matmul(ps_o[:, :], ones_f, diag[:, 0:SEQ], start=True, stop=True)
            pe.matmul(ps_m[:, 0:NB], ones_f[0:NB, :], diag[0:NB, SEQ:NT], start=True,
                      stop=True).then_inc(w_used, 1)
            pe.wait_ge(x_lo_done, 17)

            def chunk(n, slot, a):
                pe.wait_ge(w_lo_done, n + 4)
                lo, hi = CHUNKS[slot]
                for k in range(lo, hi):
                    whi, wlo = w_hi[:, slot, k - lo, :], w_lo[:, slot, k - lo, :]
                    for i, (w, m) in enumerate(((whi, mov_hi), (whi, mov_lo), (wlo, mov_hi))):
                        for h in range(2):
                            mm = pe.matmul(pj[a][h][:, 0:HT], w, m[:, k, HT * h:HT * h + HT],
                                           start=(k == 0 and i == 0), stop=(k == KT - 1 and i == 2))
                mm.then_inc(w_used, 1)

            def turn(dst, src, n=P):
                return pe.transpose(dst, src, ident[0:n, 0:n])

            def score(pr, h, u):
                pe.wait_ge(qk_split, 2 * pr + h + 1)
                if u > 0 or h > 0:
                    pe.wait_ge(biased, 8 * pr + 4 * h + (0, 2, 3)[u])
                for i, at in UNITS[u]:
                    n = P * (i + 1)
                    pe.matmul(ps_s[:, at:at + n], q_hl[:, P * i:P * i + P], k_hh[:, 0:n],
                              start=True, stop=False)
                    mm = pe.matmul(ps_s[:, at:at + n], q_hl[:, P * i:P * i + P], k_ll[:, 0:n],
                                   start=False, stop=True)
                mm.then_inc(scores, 1)

            def turn_p(pr, h, u):
                r = 3 * h + u
                pe.wait_ge(normed, 6 * pr + r + 1)
                if r > 0:
                    pe.wait_ge(pt_split, 6 * pr + r)
                for i, at in UNITS[u]:
                    for b in range(i + 1):
                        tr = turn(ps_t[:, at + P * b:at + P * b + P],
                                  pbuf[r % 2][:, at + P * b:at + P * b + P])
                tr.then_inc(p_turned, 1)

            def pv(pr, h):
                pe.wait_ge(pt_split, 6 * pr + 3 * h + 3)
                pe.wait_ge(v_split, pr + 1)
                if h == 1:
                    pe.wait_ge(o_done, 2 * pr + 1)
                for j in range(QT):
                    v = v_hl[:, j, 2 * E * h:2 * E * h + 2 * E]
                    pe.matmul(ps_o[:, P * j:SEQ], v, pt_hi[:, j, P * j:SEQ], start=(j == 0),
                              stop=False)
                    mm = pe.matmul(ps_o[:, P * j:SEQ], v, pt_lo[:, j, P * j:SEQ], start=False,
                                   stop=(j == QT - 1))
                mm.then_inc(pv_done, 1)

            with pe.Fori(0, GROUPS) as g:
                for half in range(2):
                    pr = 2 * g + half
                    for j in range(NCH):
                        tile = TPB * g + 6 * half + j // 3
                        if j % 3 == 0:
                            pe.wait_ge(tile_out, tile + 1)
                        chunk(NCH * pr + j, j % 3, (j // 3) % 2)
                        if j == 6:
                            pe.wait_ge(tile_out, TPB * g + 6 * half + 4)
                            turn(ps_m[0:NB, 0:P], z_q[:, SEQ:NT])
                            turn(ps_m[0:NB, P:2 * P], z_k[:, SEQ:NT]).then_inc(qk_rows_t, 1)
                        if j in (7, 8, 9):
                            score(pr, 0, j - 7)
                        if j == 7:
                            pe.wait_ge(qk_rows_c, pr + 1)
                            for t in range(QT):
                                tr = turn(ps_m[:, P * t:P * t + P], z_k[:, P * t:P * t + P])
                            tr.then_inc(k_nat_t, 1)
                        if j == 9:
                            pe.wait_ge(k_nat_c, pr + 1)
                            pe.wait_ge(tile_out, TPB * g + 6 * half + 5)
                            for t in range(QT):
                                tr = turn(ps_m[:, P * t:P * t + P], z_v[:, P * t:P * t + P])
                            tr.then_inc(v_nat_t, 1)
                        if j in (9, 10, 11):
                            turn_p(pr, 0, j - 9)
                        if j == 10:
                            pe.wait_ge(v_nat_c, pr + 1)
                            turn(ps_m[0:NB, 0:P], z_v[:, SEQ:NT]).then_inc(v_rows_t, 1)
                        if j == 11:
                            pe.wait_ge(v_rows_c, pr + 1)
                            pe.wait_ge(st_in, 16 * pr + 16)
                            n = NB * HIST
                            turn(ps_m[:, 0:n], st_nat[0:n, :], n).then_inc(st_t, 1)
                        if j in (11, 12, 13):
                            score(pr, 1, j - 11)
                        if j == 12:
                            pv(pr, 0)
                            pe.wait_ge(st_c, pr + 1)
                            pe.wait_ge(ns_done, pr + 1)
                            for t in range(3):
                                tr = turn(ps_m[0:16, P * t:P * t + P], ns_s[:, 16 * t:16 * t + 16])
                            tr.then_inc(ns_t, 1)
                        if j == 13:
                            pe.wait_ge(tab_in, 16)
                            pe.wait_ge(nr_s, pr + 1)
                            for t in range(3):
                                tr = turn(ps_m[:, 16 * t:16 * t + 16], p_s[0:16, P * t:P * t + P], 16)
                            tr.then_inc(pt_s_t, 1)
                        if j in (13, 14, 15):
                            turn_p(pr, 1, j - 13)
                        if j == 14:
                            pe.wait_ge(pt_s_c, pr + 1)
                            turn(ps_m[0:HIST, 0:P], lev[0][:, 16 + SEQ - HIST:16 + SEQ])
                            turn(ps_m[0:NB, P:2 * P], lev[0][:, 31 + SEQ:LW:16]).then_inc(u_rows_t, 1)
                        if j == 16:
                            pv(pr, 1)
                        if j == 17:
                            pe.wait_ge(u_rows_c, pr + 1)
                            pe.wait_ge(av_split, pr + 1)
                            for b, dst in ((0, ps_m), (1, ps_s)):
                                cols = slice(512 * b, 512 * b + 512)
                                pe.matmul(dst[:, :], ones_r[:, :], av_hi[:, cols], start=True,
                                          stop=False)
                                pe.matmul(dst[:, :], ones_r[:, :], av_lo[:, cols], start=False,
                                          stop=True).then_inc(av_sum, 1)
                for dt in range(2):
                    tile = TPB * g + 12 + dt
                    pe.wait_ge(tile_out, tile + 1)
                    pe.wait_ge(pw_split, g + 1)
                    pe.wait_ge(pooled_split, 2 * g + 2)
                    for ct in range(2):
                        whi = pw_hi[:, ct, P * dt:P * dt + P]
                        wlo = pw_lo[:, ct, P * dt:P * dt + P]
                        for i, (w, m) in enumerate(((whi, pooled_hi), (whi, pooled_lo),
                                                    (wlo, pooled_hi))):
                            for h in range(2):
                                mm = pe.matmul(pj[dt][h][:, 0:HT], w, m[:, ct, HT * h:HT * h + HT],
                                               start=(ct == 0 and i == 0), stop=(ct == 1 and i == 2))
                    mm.then_inc(tile_done, 1)

            def turn_y(d, q):
                pe.wait_ge(yt_done, d + 1)
                if not (isinstance(d, int) and d == 0):
                    pe.wait_ge(y_added, d)
                for t in range(QT):
                    turn(ps_t[:, P * t:P * t + P], y_t[q][:, P * t:P * t + P])
                turn(ps_m[0:NB, 0:P], y_t[q][:, SEQ:NT]).then_inc(y_turned, 1)

            for d in range(2):
                pe.wait_ge(tile_out, IN_TILES + d + 1)
                for c in range(3):
                    if d == 0:
                        pe.wait_ge(m_split, CHUNKS[c][1])
                    chunk(IN_CHUNKS + 3 * d + c, c, d)
                    if d == 1 and c == 0:
                        turn_y(0, 0)
            with pe.Fori(0, KT // 2 - 1) as i:
                for q in range(2):
                    d = 2 * i + q + 2
                    pe.wait_ge(yt_done, d - 1)
                    for c in range(3):
                        chunk(IN_CHUNKS + 3 * d + c, c, q)
                        if c == 0:
                            turn_y(d - 1, 1 - q)
            turn_y(KT - 1, 1)

        @block.scalar
        def _(act):
            banks = [pj[0][0], pj[0][1], pj[1][0], pj[1][1]]
            act.wait_ge(cleared, 1)
            for t in range(QT + 1):
                n = P if t < QT else NB
                act.wait_ge(x_in[t], 16)
                if t > 0:
                    act.wait_ge(squared, t)
                act.activation(junk[0:n, :], x_nat[t][0:n, :], ACT.Square,
                               accum_out=ss[0:n, t:t + 1]).then_inc(squared, 1)
                for u in range(4 * t, 4 * t + 4 if t < QT else 4 * t + 1):
                    act.wait_ge(x_turned, u + 1)
                    if t < QT:
                        src = banks[u % 4][:, :].rearrange("p (k x) -> p k x", k=4)
                        dst = mov_hi[:, 4 * (u % 4):4 * (u % 4) + 4, P * t:P * t + P]
                    else:
                        src = banks[0][:, 0:NB * KT].rearrange("p (k x) -> p k x", k=KT)
                        dst = mov_hi[:, :, SEQ:NT]
                    act.activation(dst, src, ACT.Copy).then_inc(x_hi_done, 1)
            act.wait_ge(ms_done, 1)
            act.activation(sd, ms, ACT.Sqrt).then_inc(sd_done, 1)

            def split_hi(n, slot, count):
                lo, hi = CHUNKS[slot]
                act.wait_ge(raw_in[slot], 16 * count)
                if not (isinstance(n, int) and n < 3):
                    act.wait_ge(w_used, n - 1)
                act.activation(w_hi[:, slot, 0:hi - lo, :], w_raw[:, slot, 0:hi - lo, :],
                               ACT.Copy).then_inc(w_hi_done, 1)

            def qk_hi(pr, h):
                own, other = slice(E * h, E * h + E), slice(E * (1 - h), E * (1 - h) + E)
                if h == 1:
                    act.wait_ge(scores, 6 * pr + 3)
                act.activation(q_hl[own, :], z_q[own, 0:SEQ], ACT.Copy)
                act.activation(k_hh[own, :], z_k[own, 0:SEQ], ACT.Copy)
                act.activation(k_hh[other, :], z_k[own, 0:SEQ], ACT.Copy).then_inc(qk_hi_done, 1)

            def exps(pr, h, u):
                for i, at in UNITS[u]:
                    act.wait_ge(biased, 8 * pr + 4 * h + i + 1)
                    n = P * (i + 1)
                    pb_ = pbuf[(3 * h + u) % 2][:, at:at + n]
                    act.activation(pb_, pb_, ACT.Exp, scale=-1.0, bias=nmax[:, i:i + 1],
                                   accum_out=den[:, i:i + 1]).then_inc(exped, 1)

            def p_hi(pr, h, u):
                act.wait_ge(p_turned, 6 * pr + 3 * h + u + 1)
                if u == 0 and h == 1:
                    act.wait_ge(pv_done, 2 * pr + 1)
                for i, at in UNITS[u]:
                    a = act.activation(pt_hi[:, 0:i + 1, P * i:P * i + P],
                                       ps_t[:, at:at + P * (i + 1)].rearrange(
                                           "p (j x) -> p j x", j=i + 1), ACT.Copy)
                a.then_inc(pt_hi_done, 1)

            def side(pr, h):
                own, other = slice(E * h, E * h + E), slice(E * (1 - h), E * (1 - h) + E)
                act.wait_ge(pv_done, 2 * pr + h + 1)
                act.activation(o_side[own, :], ps_o[other, :], ACT.Copy).then_inc(side_done, 1)

            for n in range(2):
                split_hi(n, n, 1)
            with act.Fori(0, GROUPS) as g:
                for half in range(2):
                    pr = 2 * g + half
                    for j in range(NCH):
                        n = j + 2
                        split_hi(NCH * pr + n, n % 3, 6 * pr + n // 3 + 1)
                        if j == 6:
                            act.wait_ge(tile_out, TPB * g + 6 * half + 4)
                            qk_hi(pr, 0)
                        if half == 1 and j == 7:
                            act.wait_ge(pw_in, 16 * g + 16)
                            act.activation(pw_hi[:, :, :], pw_raw, ACT.Copy).then_inc(pw_hi_done, 1)
                        if j == 8:
                            act.wait_ge(k_nat_t, pr + 1)
                            act.activation(k_nat, ps_m[:, :], ACT.Copy).then_inc(k_nat_c, 1)
                        if j in (8, 9, 10):
                            exps(pr, 0, j - 8)
                        if j == 10:
                            act.wait_ge(v_nat_t, pr + 1)
                            act.activation(v_nat, ps_m[:, :], ACT.Copy).then_inc(v_nat_c, 1)
                            qk_hi(pr, 1)
                        if j in (10, 11, 12):
                            p_hi(pr, 0, j - 10)
                        if j == 11:
                            act.wait_ge(v_nat_c, pr + 1)
                            for h, at in ((0, 0), (1, 3 * E)):
                                a = act.activation(
                                    v_hl[:, :, at:at + E],
                                    v_nat.rearrange("p (t h e) -> p t h e", t=QT, h=2)[:, :, h],
                                    ACT.Copy)
                            a.then_inc(v_hi_done, 1)
                        if j in (12, 13, 14):
                            exps(pr, 1, j - 12)
                        if j == 13:
                            act.wait_ge(mx_s, pr + 1)
                            act.activation(p_s[0:16, :], ps_m[0:16, 0:3 * P], ACT.Exp, scale=-1.0,
                                           bias=nmax_s, accum_out=den_s).then_inc(ex_s, 1)
                            side(pr, 0)
                        if j in (14, 15, 16):
                            p_hi(pr, 1, j - 14)
                        if j == 15:
                            act.wait_ge(tile_out, TPB * g + 6 * half + 7)
                            act.activation(th, z_gp[half], ACT.Tanh, scale=0.5).then_inc(gp_tanh, 1)
                        if j == 17:
                            act.wait_ge(mean_done, 3 * pr + 3)
                            act.activation(pooled_hi[:, half, :], pooled,
                                           ACT.Copy).then_inc(pooled_hi_done, 1)
                            side(pr, 1)
                            act.wait_ge(av_add, 2 * pr + 2)
                            act.activation(av_hi[:, :], kv[:, 0, :], ACT.Copy).then_inc(av_hi_done, 1)
                    act.wait_ge(tile_out, TPB * g + 6 * half + 8)
                    act.wait_ge(gp_gate, pr + 1)
                    act.activation(th, z_ga, ACT.Tanh, scale=0.5).then_inc(ga_tanh, 1)

            act.wait_ge(w_used, IN_CHUNKS + 1)
            for k in range(KT):
                act.wait_ge(mix_back[k % 3], 16 * (k // 3 + 1))
                act.activation(mov_hi[:, k, :], mix_in[k % 3], ACT.Copy).then_inc(m_hi_done, 1)

            def y_out(d, q):
                act.wait_ge(w_used, IN_CHUNKS + 3 * d + 4)
                if not (isinstance(d, int) and d < 2):
                    act.wait_ge(y_turned, d - 1)
                act.activation(y_t[q][:, 0:HT], pj[q][0][:, 0:HT], ACT.Copy)
                act.activation(y_t[q][:, HT:NT], pj[q][1][:, 0:HT], ACT.Copy).then_inc(yt_done, 1)

            def y_square(d):
                act.wait_ge(y_added, d + 1)
                for t in range(QT + 1):
                    n = P if t < QT else NB
                    src = y[:, t, bass.ds(P * d, P)] if t < QT else y_s[0:NB, bass.ds(P * d, P)]
                    if not (isinstance(d, int) and d == 0 and t == 0):
                        act.wait_ge(y_sq, 5 * d + t)
                    act.activation(sq_junk[0:n, :], src, ACT.Square,
                                   accum_out=ss_y[0:n, t, bass.ds(d, 1)]).then_inc(y_sq, 1)

            def out_pos(d, q, chunks=3):
                if not (isinstance(d, int) and d == 0):
                    y_out(d - 1, 1 - q)
                for c in range(chunks):
                    n = 3 * d + c + 2
                    split_hi(IN_CHUNKS + n, (c + 2) % 3, 6 * PAIRS + d + (c + 2) // 3 + 1)
                if not (isinstance(d, int) and d == 0):
                    y_square(d - 1)

            out_pos(0, 0)
            out_pos(1, 1)
            with act.Fori(0, KT // 2 - 2) as i:
                for q in range(2):
                    out_pos(2 * i + q + 2, q)
            out_pos(KT - 2, 0)
            out_pos(KT - 1, 1, chunks=1)
            y_out(KT - 1, 1)
            y_square(KT - 1)
            act.wait_ge(f_ms, 1)
            act.activation(sd, ms, ACT.Sqrt).then_inc(f_sd, 1)

        @block.gpsimd
        def _(pool):
            with pool.Fori(0, GROUPS) as g:
                for half in range(2):
                    pr = 2 * g + half
                    cols = bass.ds(P * pr, P)
                    pool.wait_ge(qk_rows_c, pr + 1)
                    pool.sem_inc(rows_seen, 1)
                    pool.dma_start(row_dram[0:2].rearrange("a b x -> b a x"),
                                   rows[0:NB, 0:2, :]).then_inc(row_wr, 16)
                    pool.dma_start(kn_out[:, cols], rows[0:NB, 1, :]).then_inc(kn_st, 16)
                    pool.wait_ge(row_wr, 16 * pr + 16)
                    pool.sem_inc(rows_seen, 1)
                    pool.dma_start(q_bc, row_dram[0].rearrange("b x -> (b x)").partition_broadcast(P)
                                   ).then_inc(q_bc_in, 16)
                    pool.dma_start(kv[96:97, 1, :], row_dram[1:2].rearrange("a b x -> a (b x)")
                                   ).then_inc(kn_in, 16)
                    pool.wait_ge(k_in, 48 * pr + 48)
                    pool.wait_ge(q_bc_in, 16 * pr + 16)
                    pool.wait_ge(kn_in, 16 * pr + 16)
                    for t, r in enumerate(ROWS_T):
                        pool.tensor_tensor(kv[0:r, t, :], kv[0:r, t, :], q_bc[0:r, :],
                                           ALU.mult).then_inc(kq_done, 1)
                    pool.wait_ge(v_rows_c, pr + 1)
                    pool.sem_inc(rows_seen, 1)
                    pool.dma_start(row_dram[2], rows[0:NB, 2, :]).then_inc(vrow_wr, 16)
                    pool.dma_start(vn_out[:, cols], rows[0:NB, 2, :]).then_inc(vn_st, 16)
                    pool.wait_ge(vrow_wr, 16 * pr + 16)
                    pool.wait_ge(kq_sum, 3 * pr + 3)
                    pool.sem_inc(rows_seen, 1)
                    pool.dma_start(kv[96:97, 1, :], row_dram[2:3].rearrange("a b x -> a (b x)")
                                   ).then_inc(vn_in, 16)
                    pool.wait_ge(kn_st, 16 * pr + 16)
                    pool.wait_ge(vn_st, 16 * pr + 16)
                    pool.wait_ge(v_in, 48 * pr + 48)
                    pool.wait_ge(vn_in, 16 * pr + 16)
                    pool.wait_ge(pt_s_c, pr + 1)
                    for t, r in enumerate(ROWS_T):
                        vt = kv[0:r, t, :].rearrange("p (bh e) -> p bh e", e=E)
                        pb_ = pt_s[0:r, 16 * t:16 * t + 16].unsqueeze(2).to_broadcast([r, 16, E])
                        pool.tensor_tensor(vt, vt, pb_, ALU.mult).then_inc(pv_s, 1)
                    pool.wait_ge(u_rows_c, pr + 1)
                    pool.dma_start(pss_out[:, HIST - 1, cols], u_rows[0:NB, 1, :]).then_inc(us_st, 16)
                    pool.dma_start(psp_out[:, cols], u_rows[0:HIST, 0, :]).then_inc(up_st, 16)
                    pool.wait_ge(us_st, 16 * pr + 16)
                    pool.wait_ge(up_st, 16 * pr + 16)
                    pool.wait_ge(mixed, pr + 1)
                    pool.dma_start(mix_dram[bass.ds(pr + PAIRS, 1)].rearrange("a p x -> (a p) x"),
                                   attn).then_inc(mix_st, 16)
                    pool.wait_ge(mix_st, 16 * pr + 16)
                for dt in range(2):
                    pool.wait_ge(tile_out, TPB * g + 15 + dt)
                    pool.dma_start(mix_dram[bass.ds(2 * g + dt, 1)].rearrange("a p x -> (a p) x"),
                                   z_gp[dt]).then_inc(pmix_st, 16)
                pool.wait_ge(pmix_st, 32 * g + 32)

        @block.vector
        def _(dve):
            def rstd_of(done):
                dve.reciprocal(rstd, sd).then_inc(done, 1)
                dve.wait_ge(done, 1)
                dve.scalar_tensor_tensor(out=sd, in0=rstd, scalar=-0.5, in1=rstd, op0=ALU.mult,
                                         op1=ALU.mult).then_inc(done, 1)
                dve.wait_ge(done, 2)
                dve.tensor_tensor(sd, sd, ms, ALU.mult).then_inc(done, 1)
                dve.wait_ge(done, 3)
                dve.scalar_tensor_tensor(out=rstd, in0=sd, scalar=1.5, in1=rstd, op0=ALU.add,
                                         op1=ALU.mult).then_inc(done, 1)
                dve.wait_ge(done, 4)

            dve.memset(stat[:, :], 0.0).then_inc(cleared, 1)
            dve.memset(ones_f, 1.0).then_inc(w_lo_done, 1)
            dve.memset(diag, 0.0).then_inc(w_lo_done, 1)
            dve.memset(ones_r[:, :].bitcast(F32), 1.0).then_inc(w_lo_done, 1)
            dve.wait_ge(g_in, 16)
            dve.wait_ge(tab_in, 16)
            banks = [pj[0][0], pj[0][1], pj[1][0], pj[1][1]]
            for t in range(QT + 1):
                n = P if t < QT else NB
                dve.wait_ge(squared, t + 1)
                dve.tensor_tensor(x_nat[t][0:n, :], x_nat[t][0:n, :], g_bc[0:n, :],
                                  ALU.mult).then_inc(scaled, 1)
                for u in range(4 * t, 4 * t + 4 if t < QT else 4 * t + 1):
                    dve.wait_ge(x_hi_done, u + 1)
                    if t < QT:
                        src = banks[u % 4][:, :].rearrange("p (k x) -> p k x", k=4)
                        at = (slice(None), slice(4 * (u % 4), 4 * (u % 4) + 4), slice(P * t, P * t + P))
                    else:
                        src = banks[0][:, 0:NB * KT].rearrange("p (k x) -> p k x", k=KT)
                        at = (slice(None), slice(None), slice(SEQ, NT))
                    dve.tensor_tensor(mov_lo[at], src, mov_hi[at].bitcast(F32),
                                      ALU.subtract).then_inc(x_lo_done, 1)
            dve.tensor_scalar(ms, ss, 1.0 / D_MODEL, EPS, ALU.mult, ALU.add).then_inc(ms_done, 1)
            dve.wait_ge(sd_done, 1)
            rstd_of(rs_done)
            for t in range(QT):
                dve.tensor_scalar(diag[:, P * t:P * t + P], ident, rstd[:, t:t + 1], None,
                                  ALU.mult).then_inc(diag_done, 1)
            dve.tensor_scalar(diag[0:NB, SEQ:NT], ident[0:NB, 0:NB], rstd[0:NB, QT:QT + 1], None,
                              ALU.mult).then_inc(diag_done, 1)

            def split_lo(n, slot):
                lo, hi = CHUNKS[slot]
                dve.wait_ge(w_hi_done, n + 1)
                dve.tensor_tensor(w_lo[:, slot, 0:hi - lo, :], w_raw[:, slot, 0:hi - lo, :],
                                  w_hi[:, slot, 0:hi - lo, :].bitcast(F32),
                                  ALU.subtract).then_inc(w_lo_done, 1)

            for n in range(2):
                split_lo(n, n)
            dve.wait_ge(w_used, 1)
            dve.tensor_copy(rstd_bc[:, 0:SEQ], ps_o[:, :]).then_inc(tile_out, 1)
            dve.tensor_copy(rstd_bc[:, SEQ:NT], ps_m[:, 0:NB]).then_inc(tile_out, 1)
            for b in lev:
                dve.memset(b[:, 0:16], 0.0)
            dve.memset(sc_s, 0.0).then_inc(cleared, 1)
            dve.wait_ge(ps_in, 16)
            dve.tensor_scalar(pscale[:, :], pscale[:, :], 0.5, None, ALU.mult).then_inc(rb_done, 1)
            dve.wait_ge(cleared, 2)
            dve.wait_ge(rb_done, 1)
            dve.wait_ge(tile_out, 2)

            def take_tile(n, a, dsts, scale=1.0):
                dve.wait_ge(w_used, n + 2)
                for i, (dst, h, c0, c1) in enumerate(dsts):
                    o = dve.scalar_tensor_tensor(out=dst, in0=pj[a][h][:, c0:c1], scalar=scale,
                                                 in1=rstd_bc[:, HT * h + c0:HT * h + c1],
                                                 op0=ALU.mult, op1=ALU.mult)
                o.then_inc(tile_out, 1)

            def whole(z):
                return [(z[:, 0:HT], 0, 0, HT), (z[:, HT:NT], 1, 0, HT)]

            def qk_lo(pr, h):
                own, other = slice(E * h, E * h + E), slice(E * (1 - h), E * (1 - h) + E)
                dve.wait_ge(qk_hi_done, 2 * pr + h + 1)
                dve.tensor_tensor(q_hl[other, :], z_q[own, 0:SEQ], q_hl[own, :].bitcast(F32),
                                  ALU.subtract)
                for dst in (own, other):
                    o = dve.tensor_tensor(k_ll[dst, :], z_k[own, 0:SEQ], k_hh[own, :].bitcast(F32),
                                          ALU.subtract)
                o.then_inc(qk_split, 1)

            def head_bias(pr, h):
                if h == 1:
                    dve.wait_ge(biased, 8 * pr + 4)
                dve.scalar_tensor_tensor(out=nbias, in0=tab[:, C_DIST:C_DIST + SEQ],
                                         scalar=tab[:, bass.ds(2 * pr + h + C_SLOPE, 1)],
                                         in1=tab[:, C_NLOG:C_NLOG + SEQ], op0=ALU.mult,
                                         op1=ALU.add).then_inc(bias_done, 1)

            def bias_unit(pr, h, u):
                dve.wait_ge(scores, 6 * pr + 3 * h + u + 1)
                dve.wait_ge(bias_done, 2 * pr + h + 1)
                r = 3 * h + u
                if r >= 2:
                    dve.wait_ge(p_turned, 6 * pr + r - 1)
                dve.sem_inc(unit_starts, 1)
                for i, at in UNITS[u]:
                    n = P * (i + 1)
                    dve.tensor_tensor_reduce(out=pbuf[r % 2][:, at:at + n],
                                             in0=ps_s[:, at:at + n], in1=nbias[:, SEQ - n:SEQ],
                                             scale=1.0, scalar=3e38, op0=ALU.add, op1=ALU.min,
                                             accum_out=nmax[:, i:i + 1]).then_inc(biased, 1)

            def norm_unit(pr, h, u):
                for i, at in UNITS[u]:
                    n = P * (i + 1)
                    dve.wait_ge(exped, 8 * pr + 4 * h + i + 1)
                    dve.reciprocal(rden[:, i:i + 1], den[:, i:i + 1]).then_inc(recip, 1)
                    dve.wait_ge(recip, 8 * pr + 4 * h + i + 1)
                    pb_ = pbuf[(3 * h + u) % 2][:, at:at + n]
                    o = dve.tensor_scalar(pb_, pb_, rden[:, i:i + 1], None, ALU.mult)
                o.then_inc(normed, 1)

            def p_lo(pr, h, u):
                dve.wait_ge(pt_hi_done, 6 * pr + 3 * h + u + 1)
                for i, at in UNITS[u]:
                    blk = (slice(None), slice(0, i + 1), slice(P * i, P * i + P))
                    o = dve.tensor_tensor(pt_lo[blk],
                                          ps_t[:, at:at + P * (i + 1)].rearrange(
                                              "p (j x) -> p j x", j=i + 1),
                                          pt_hi[blk].bitcast(F32), ALU.subtract)
                o.then_inc(pt_split, 1)

            def head_out(pr, h):
                own = slice(E * h, E * h + E)
                dve.wait_ge(side_done, 2 * pr + h + 1)
                dve.tensor_tensor(attn[own, 0:SEQ], ps_o[own, :], o_side[own, :],
                                  ALU.add).then_inc(o_done, 1)

            samp = slice(31 + SEQ, LW, 16)
            with dve.Fori(0, GROUPS) as g:
                for half in range(2):
                    pr = 2 * g + half
                    ch = NCH * pr
                    t0 = TPB * g + 6 * half
                    for j in range(NCH):
                        if j == 3:
                            take_tile(ch + 2, 0, whole(z_q), -SCALE)
                        if j == 6:
                            take_tile(ch + 5, 1, whole(z_k))
                        if j == 9:
                            take_tile(ch + 8, 0, whole(z_v))
                        if j == 12:
                            take_tile(ch + 11, 1, [
                                (lev[0][:, 16:16 + HT], 0, 0, HT),
                                (lev[0][:, 16 + HT:16 + SEQ], 1, 0, SEQ - HT),
                                (lev[0][:, samp], 1, SEQ - HT, HT)])
                        if j == 15:
                            take_tile(ch + 14, 0, whole(z_gp[half]))
                        split_lo(ch + j + 2, (j + 2) % 3)
                        if j == 6:
                            dve.wait_ge(tile_out, t0 + 4)
                            qk_lo(pr, 0)
                        if j == 7:
                            head_bias(pr, 0)
                            dve.wait_ge(qk_rows_t, pr + 1)
                            dve.tensor_copy(rows[0:NB, 0:2, :], ps_m[0:NB, 0:2 * P].rearrange(
                                "p (a x) -> p a x", a=2)).then_inc(qk_rows_c, 1)
                        if j in (9, 10, 11):
                            norm_unit(pr, 0, j - 9)
                        if j in (8, 9, 10):
                            bias_unit(pr, 0, j - 8)
                        if half == 1 and j == 8:
                            dve.wait_ge(pw_hi_done, g + 1)
                            dve.tensor_tensor(pw_lo[:, :, :], pw_raw, pw_hi[:, :, :].bitcast(F32),
                                              ALU.subtract).then_inc(pw_split, 1)
                        if j in (10, 11, 12):
                            p_lo(pr, 0, j - 10)
                        if j == 10:
                            qk_lo(pr, 1)
                        if j == 11:
                            dve.wait_ge(v_hi_done, pr + 1)
                            vn = v_nat.rearrange("p (t x) -> p t x", t=QT)
                            for h in range(2):
                                vh = v_hl[:, :, 3 * E * h:3 * E * h + E].bitcast(F32)
                                o = dve.tensor_tensor(v_hl[:, :, E * (1 + h):E * (2 + h)],
                                                      vn[:, :, E * h:E * h + E], vh, ALU.subtract)
                            o.then_inc(v_split, 1)
                            head_bias(pr, 1)
                            dve.wait_ge(v_rows_t, pr + 1)
                            dve.tensor_copy(rows[0:NB, 2, :], ps_m[0:NB, 0:P]).then_inc(v_rows_c, 1)
                            for t, r in enumerate(ROWS_T):
                                dve.wait_ge(kq_done, 3 * pr + t + 1)
                                dve.tensor_reduce(sc_s[0:r, 16 * t:16 * t + 16],
                                                  kv[0:r, t, :].rearrange("p (x e) -> p x e", e=E),
                                                  AX_X, ALU.add).then_inc(kq_sum, 1)
                            dve.wait_ge(kq_sum, 3 * pr + 3)
                            sbt = tab[:, C_SB:C_SB + 48].rearrange("p (t h) -> p t h", t=3)[
                                :, :, bass.ds(2 * pr, 2)].unsqueeze(2).to_broadcast([P, 3, NB, 2])
                            dve.tensor_tensor(ns_s.rearrange("p (t b h) -> p t b h", t=3, b=NB),
                                              sc_s.rearrange("p (t b h) -> p t b h", t=3, b=NB),
                                              sbt, ALU.add).then_inc(ns_done, 1)
                        if j == 12:
                            dve.wait_ge(st_t, pr + 1)
                            dve.tensor_copy(
                                lev[0][:, 16 + SEQ:LW].rearrange("p (b s) -> p b s", b=NB)[:, :, 0:HIST],
                                ps_m[:, 0:NB * HIST].rearrange("p (b s) -> p b s", b=NB)
                            ).then_inc(st_c, 1)
                        if j in (13, 14, 15):
                            norm_unit(pr, 1, j - 13)
                        if j in (12, 13, 14):
                            bias_unit(pr, 1, j - 12)
                        if j == 13:
                            dve.wait_ge(ns_t, pr + 1)
                            dve.tensor_reduce(nmax_s, ps_m[0:16, 0:3 * P], AX_X,
                                              ALU.min).then_inc(mx_s, 1)
                            head_out(pr, 0)
                            dve.wait_ge(ex_s, pr + 1)
                            dve.reciprocal(rden_s, den_s).then_inc(rc_s, 1)
                            dve.wait_ge(rc_s, pr + 1)
                            dve.tensor_scalar(p_s[0:16, :], p_s[0:16, :], rden_s, None,
                                              ALU.mult).then_inc(nr_s, 1)
                        if j in (14, 15, 16):
                            p_lo(pr, 1, j - 14)
                        if j == 14:
                            dve.wait_ge(pt_s_t, pr + 1)
                            dve.tensor_copy(pt_s, ps_m[:, 0:48]).then_inc(pt_s_c, 1)
                            dve.wait_ge(st_c, pr + 1)
                            dve.wait_ge(tile_out, t0 + 6)
                            dve.tensor_tensor(lev[1][:, 16:LW], lev[0][:, 16:LW],
                                              lev[0][:, 15:LW - 1], ALU.add).then_inc(lev_done, 1)
                        if j in (14, 15):
                            for i in ((0,) if j == 14 else (1, 2)):
                                s, src, dst = 2 << i, lev[1 + i % 2], lev[2 - i % 2]
                                dve.wait_ge(lev_done, 4 * pr + i + 1)
                                dve.scalar_tensor_tensor(
                                    out=dst[:, 16:LW], in0=src[:, 16 - s:LW - s],
                                    scalar=tab[:, bass.ds(3 * g + i + C_LM, 1)], in1=src[:, 16:LW],
                                    op0=ALU.mult, op1=ALU.add).then_inc(lev_done, 1)
                        if j == 15:
                            dve.wait_ge(u_rows_t, pr + 1)
                            dve.tensor_copy(u_rows[0:NB, 1, :], ps_m[0:NB, P:2 * P])
                            dve.tensor_copy(u_rows[0:HIST, 0, :], ps_m[0:HIST, 0:P]).then_inc(u_rows_c, 1)
                        if j == 16:
                            total, iw = lev[2], tab[:, bass.ds(g + C_IW, 1)]
                            dve.wait_ge(lev_done, 4 * pr + 4)
                            dve.tensor_tensor(t16, total[:, 16:32],
                                              tab[:, bass.ds(16 * g + C_INV, 16)],
                                              ALU.mult).then_inc(mean_done, 1)
                            dve.scalar_tensor_tensor(out=pooled[:, 16:SEQ], in0=total[:, 32:16 + SEQ],
                                                     scalar=iw, in1=lev[0][:, 32:16 + SEQ],
                                                     op0=ALU.mult, op1=ALU.subtract)
                            dve.scalar_tensor_tensor(out=pooled[:, SEQ:NT], in0=total[:, samp],
                                                     scalar=iw, in1=lev[0][:, samp], op0=ALU.mult,
                                                     op1=ALU.subtract).then_inc(mean_done, 1)
                            dve.wait_ge(mean_done, 3 * pr + 2)
                            dve.tensor_tensor(pooled[:, 0:16], t16, lev[0][:, 16:32],
                                              ALU.subtract).then_inc(mean_done, 1)
                            dve.wait_ge(gp_tanh, pr + 1)
                            dve.scalar_tensor_tensor(out=z_gp[half], in0=th, scalar=1.0,
                                                     in1=z_gp[half], op0=ALU.add,
                                                     op1=ALU.mult).then_inc(gp_gate, 1)
                        if j == 17:
                            dve.wait_ge(pv_s, 3 * pr + 3)
                            for t in (1, 2):
                                r = ROWS_T[t]
                                if t == 2:
                                    dve.wait_ge(av_add, 2 * pr + 1)
                                dve.tensor_tensor(kv[0:r, 0, :], kv[0:r, 0, :], kv[0:r, t, :],
                                                  ALU.add).then_inc(av_add, 1)
                            dve.wait_ge(pooled_hi_done, pr + 1)
                            dve.tensor_tensor(pooled_lo[:, half, :], pooled,
                                              pooled_hi[:, half, :].bitcast(F32),
                                              ALU.subtract).then_inc(pooled_split, 1)
                            head_out(pr, 1)
                            dve.wait_ge(av_hi_done, pr + 1)
                            dve.tensor_tensor(av_lo[:, :], kv[:, 0, :], av_hi[:, :].bitcast(F32),
                                              ALU.subtract).then_inc(av_split, 1)
                    take_tile(ch + 17, 1, whole(z_ga))
                    for b, src in ((0, ps_m), (1, ps_s)):
                        dve.wait_ge(av_sum, 2 * pr + b + 1)
                        if b == 1:
                            dve.wait_ge(pick, 4 * pr + 2)
                        tmp = nbias.rearrange("p (b e) -> p b e", b=4)
                        dve.tensor_tensor(tmp, src[:, :].rearrange("p (b e) -> p b e", b=4),
                                          ident.unsqueeze(1).to_broadcast([P, 4, P]),
                                          ALU.mult).then_inc(pick, 1)
                        dve.wait_ge(pick, 4 * pr + 2 * b + 1)
                        dve.tensor_reduce(attn[:, SEQ + 4 * b:SEQ + 4 * b + 4], tmp, AX_X,
                                          ALU.add).then_inc(pick, 1)
                    dve.wait_ge(pick, 4 * pr + 4)
                    dve.wait_ge(o_done, 2 * pr + 2)
                    dve.wait_ge(ga_tanh, pr + 1)
                    dve.scalar_tensor_tensor(out=z_ga, in0=th, scalar=1.0, in1=z_ga, op0=ALU.add,
                                             op1=ALU.mult).then_inc(ga_gate, 1)
                    dve.wait_ge(ga_gate, pr + 1)
                    dve.scalar_tensor_tensor(out=attn, in0=attn, scalar=0.5, in1=z_ga, op0=ALU.mult,
                                             op1=ALU.mult).then_inc(mixed, 1)
                for dt in range(2):
                    dve.wait_ge(tile_done, 2 * g + dt + 1)
                    for h in range(2):
                        c = slice(HT * h, HT * h + HT)
                        o = dve.scalar_tensor_tensor(
                            out=z_gp[dt][:, c], in0=pj[dt][h][:, 0:HT],
                            scalar=pscale[:, bass.ds(2 * g + dt, 1)], in1=z_gp[dt][:, c],
                            op0=ALU.mult, op1=ALU.mult)
                    o.then_inc(tile_out, 1)

            for k in range(KT):
                dve.wait_ge(m_hi_done, k + 1)
                dve.tensor_tensor(mov_lo[:, k, :], mix_in[k % 3], mov_hi[:, k, :].bitcast(F32),
                                  ALU.subtract).then_inc(m_split, 1)

            def add_res(d, q, count):
                dve.wait_ge(y_turned, d + 1)
                dve.wait_ge(xr_in[q], 16 * count + 16)
                dve.wait_ge(xrs_in[q], 16 * count + 16)
                dve.tensor_tensor(y[:, :, bass.ds(P * d, P)],
                                  ps_t[:, :].rearrange("p (t x) -> p t x", t=QT),
                                  x_res[q][:, 0:SEQ].rearrange("p (t x) -> p t x", t=QT), ALU.add)
                dve.tensor_tensor(y_s[0:NB, bass.ds(P * d, P)], ps_m[0:NB, 0:P],
                                  x_res[q][0:NB, SEQ:SEQ + P], ALU.add).then_inc(y_added, 1)

            def out_pos(d, q, count, chunks=3):
                for c in range(chunks):
                    split_lo(IN_CHUNKS + 3 * d + c + 2, (c + 2) % 3)
                if not (isinstance(d, int) and d == 0):
                    add_res(d - 1, 1 - q, count)

            out_pos(0, 0, 0)
            dve.memset(ss_y, 0.0).then_inc(cleared, 1)
            out_pos(1, 1, 0)
            with dve.Fori(0, KT // 2 - 2) as i:
                for q in range(2):
                    out_pos(2 * i + q + 2, q, i + q)
            out_pos(KT - 2, 0, KT // 2 - 2)
            out_pos(KT - 1, 1, KT // 2 - 1, chunks=1)
            add_res(KT - 1, 1, KT // 2 - 1)
            dve.wait_ge(y_sq, 5 * KT)
            dve.tensor_reduce(ss, ss_y, AX_X, ALU.add).then_inc(f_sum, 1)
            dve.wait_ge(f_sum, 1)
            dve.tensor_scalar(ms, ss, 1.0 / D_MODEL, EPS, ALU.mult, ALU.add).then_inc(f_ms, 1)
            dve.wait_ge(f_sd, 1)
            rstd_of(f_rs)
            dve.wait_ge(gf_in, 16)
            for t in range(QT + 1):
                n = P if t < QT else NB
                yt = y[:, t, :] if t < QT else y_s[0:NB, :]
                dve.scalar_tensor_tensor(out=yt, in0=yt, scalar=rstd[0:n, t:t + 1],
                                         in1=gf_bc[0:n, :], op0=ALU.mult,
                                         op1=ALU.mult).then_inc(f_out, 1)

    return nc


INS = ("x_prompt", "x_sample", "state_pool", "cache_k_win", "cache_v_win", "norm_g", "w_in",
       "pool_w", "pool_scale", "w_out", "final_norm_g")
OUTS = ((1, SEQ, D_MODEL), (NB, 1, D_MODEL), (1, 1, HIST, D_HALF), (1, 1, SEQ, HEADS, E),
        (1, 1, SEQ, HEADS, E), (1, NB, HIST, D_HALF), (1, NB, 1, HEADS, E), (1, NB, 1, HEADS, E))


def kernel(**inputs):
    import concourse.bacc as bacc
    from concourse.bass_utils import run_bass_kernel_spmd

    nc = bacc.Bacc("TRN2", target_bir_lowering=False, num_devices=1)
    arrays, args = {}, []
    for name in INS:
        a = np.ascontiguousarray(inputs[name])
        arrays[f"in_{name}"] = a
        args.append(nc.dram_tensor(f"in_{name}", a.shape, mybir.dt.from_np(a.dtype),
                                   kind="ExternalInput").ap())
    arrays["in_tables"] = constants()
    args.append(nc.dram_tensor("in_tables", (P, C_END), F32, kind="ExternalInput").ap())
    for i, shape in enumerate(OUTS):
        args.append(nc.dram_tensor(f"out_{i}", shape, F32, kind="ExternalOutput").ap())
    layer_step(nc, *args)
    r = run_bass_kernel_spmd(nc, [arrays], core_ids=[0])
    return tuple(r.results[0][f"out_{i}"] for i in range(len(OUTS)))
```

```python
from contextlib import ExitStack

import concourse.bass as bass
import numpy as np
from concourse import mybir
from concourse.alu_op_type import AluOpType as ALU

F32 = mybir.dt.float32
F32R = mybir.dt.float32r
ACT = mybir.ActivationFunctionType
AX_X = mybir.AxisListType.X

P = 128
D_MODEL = 2048
SEQ = 512
NB = 8
NT = SEQ + NB
HT = NT // 2
D_HALF = 1024
HEADS, E = 16, 64
PAIRS = HEADS // 2
GROUPS = 4
WINDOWS = (2, 4, 8, 16)
PAST = 2048
HIST = 15
KT = D_MODEL // P
CHUNKS = ((0, 6), (6, 11), (11, 16))
CK = 6
SLOTS = 3
NCH = 18
COL_OF = (2048, 3072, 4096, 0, 1024, 5120)
TPB = 14
QT = SEQ // P
ROWS_T = (128, 97, 96)
LW = 16 + SEQ + 16 * NB
SCALE = float(E) ** -0.5
EPS = 1e-6
MASKED = 1e30

RELOADED = (0, 1, 2, 3, 4, 5, 8, 9, 10, 11, 12, 13, 14)
MIX_BUFS = 6
POOL_SPLITS = (3, 5, 7, 8, 9, 10)

UNITS = (((0, 0), (1, 128)), ((2, 0),), ((3, 0),))

C_ID, C_DIST, C_NLOG, C_SLOPE, C_SB, C_INV, C_IW, C_LM, C_END = np.cumsum(
    [0, 128, 512, 512, 16, 48, 64, 4, 12]).tolist()


def constants():
    t = np.zeros((P, C_END), np.float32)
    t[:, C_ID:C_ID + P] = np.eye(P, dtype=np.float32)

    def count(d):
        return ((d >= 0) & (d <= 128)) * 1 + ((d >= 0) & (d <= 512) & (d % 4 == 0)) * 1 + \
            ((d >= 0) & (d <= 2048) & (d % 16 == 0)) * 1

    def neg_log(c):
        return np.where(c > 0, -np.log(np.maximum(c, 1)), MASKED)

    d = np.arange(P)[:, None] + 384 - np.arange(SEQ)[None, :]
    c = count(d)
    t[:, C_DIST:C_DIST + SEQ] = np.where(c > 0, d, 0)
    t[:, C_NLOG:C_NLOG + SEQ] = neg_log(c)
    slopes = (2.0 ** (-8.0 * np.arange(1, HEADS + 1) / HEADS)).astype(np.float32)
    t[:, C_SLOPE:C_SLOPE + HEADS] = slopes
    p = np.arange(P)
    ds = np.stack([128 - p, 512 - 4 * p, 2048 - 16 * p], 1)
    ds[96, 1] = 0
    live = np.stack([p < r for r in ROWS_T], 1)
    cs = np.where(live, count(ds), 0)
    sb = np.where(live, ds, 0)[:, :, None].astype(np.float32) * slopes + neg_log(cs)[:, :, None]
    t[:, C_SB:C_SB + 48] = sb.reshape(P, 48)
    for g, w in enumerate(WINDOWS):
        t[:, C_INV + 16 * g:C_INV + 16 * g + 16] = 1.0 / np.minimum(w, np.arange(16) + 1)
        t[:, C_IW + g] = 1.0 / w
        for j in range(3):
            t[:, C_LM + 3 * g + j] = 1.0 if j + 1 <= g else 0.0
    return t


def layer_step(nc, x_prompt, x_sample, state_pool, cache_k, cache_v, norm_g, w_in, pool_w,
               pool_scale, w_out, final_g, consts, y_prompt, y_sample, pool_state_p, k_win_p,
               v_win_p, pool_state_s, k_new, v_new):
    with ExitStack() as ctx:
        def sb(name, shape, dt=F32):
            return ctx.enter_context(nc.sbuf_tensor(name, shape, dt))

        def bank(name):
            return ctx.enter_context(nc.psum_tensor(name, [P, 512], F32))

        def sem(name):
            return ctx.enter_context(nc.semaphore(name))

        xp = x_prompt.rearrange("b (t p) d -> (b p) t d", p=P)
        xs = x_sample.rearrange("b s d -> (b s) d")
        wi = w_in.rearrange("l (k p) e -> (l p) k e", p=P)
        wo = w_out.rearrange("l (k p) e -> (l p) k e", p=P)
        pw = pool_w.rearrange("l g (c p) d -> (l g) p c d", p=P)

        def cache_rows(c):
            rows = c.rearrange("l b r h e -> (l b) r (h e)")

            def every(lo, hi, step):
                return rows[:, lo:hi, :].rearrange("b (r s) x -> r s b x", s=step)[:, 0]
            return every(1920, 2048, 1), every(1536, 1920, 4), every(0, 1536, 16)
        k_rows, v_rows = cache_rows(cache_k), cache_rows(cache_v)
        st = state_pool.rearrange("l b s c -> (l b s) c")
        k_out = k_win_p.rearrange("l b (t p) h e -> (l b p) t (h e)", p=P)
        v_out = v_win_p.rearrange("l b (t p) h e -> (l b p) t (h e)", p=P)
        kn_out = k_new.rearrange("l b s h e -> (l b s) (h e)")
        vn_out = v_new.rearrange("l b s h e -> (l b s) (h e)")
        psp_out = pool_state_p.rearrange("l b s c -> (l b s) c")
        pss_out = pool_state_s.rearrange("l b s c -> (l b) s c")
        pss_in = state_pool.rearrange("l b s c -> (l b) s c")
        yp = y_prompt.rearrange("b (t p) d -> (b p) t d", p=P)
        ys_out = y_sample.rearrange("b s d -> (b s) d")
        mix_dram = nc.dram_tensor("mix_scratch", [KT, P, NT], F32, kind="Internal").ap()
        rstd_dram = nc.dram_tensor("rstd_scratch", [NT], F32, kind="Internal").ap()
        row_dram = nc.dram_tensor("row_scratch", [3, NB, P], F32, kind="Internal").ap()

        mov_hi = sb("mov_hi", [P, KT, NT], F32R)
        mov_lo = sb("mov_lo", [P, KT, NT], F32R)
        w_hi = sb("w_hi", [P, SLOTS, CK, P], F32R)
        w_lo = sb("w_lo", [P, SLOTS, CK, P], F32R)
        q_hl = sb("q_hl", [P, SEQ], F32R)
        k_hh = sb("k_hh", [P, SEQ], F32R)
        k_ll = sb("k_ll", [P, SEQ], F32R)
        pt_hi = sb("pt_hi", [P, QT, SEQ], F32R)
        pt_lo = sb("pt_lo", [P, QT, SEQ], F32R)
        v_hl = sb("v_hl", [P, QT, 4 * E], F32R)
        pooled_hi = sb("pooled_hi", [P, 2, NT], F32R)
        pooled_lo = sb("pooled_lo", [P, 2, NT], F32R)
        pw_hi = sb("pw_hi", [P, 2, 256], F32R)
        pw_lo = sb("pw_lo", [P, 2, 256], F32R)
        av_hi = sb("av_hi", [P, NB * P], F32R)
        av_lo = sb("av_lo", [P, NB * P], F32R)
        ones_r = sb("ones_r", [P, P], F32R)

        w_raw = sb("w_raw", [P, SLOTS, CK, P])
        tab = sb("tab", [P, C_END])
        rstd_bc = sb("rstd_bc", [P, NT])
        stat = sb("stat", [P, 40])
        pscale = sb("pscale", [P, PAIRS])
        arena = sb("arena", [P, 15856])

        ident = tab[:, C_ID:C_ID + P]

        def carver():
            at = [0]

            def take(n):
                at[0] += n
                assert at[0] <= 15856, at[0]
                return arena[:, at[0] - n:at[0]]
            return take
        take = carver()
        x_nat = take(QT * D_MODEL).rearrange("p (t d) -> p t d", t=QT)
        x_smp = take(D_MODEL)
        junk_a = [take(SEQ) for _ in range(2)]
        junk_l = [take(D_MODEL), x_smp]
        junk_p = take(D_MODEL)
        g_rows, g_t = take(P), take(KT)
        xg_smp = take(NB * KT)
        ss_x = take((QT + 1) * QT).rearrange("p (t c) -> p t c", t=QT + 1)
        take = carver()
        z_q, z_k, z_v = take(NT), take(NT), take(NT)
        k_nat, v_nat = take(SEQ), take(SEQ)
        pbuf = [take(SEQ), take(SEQ)]
        z_gp = [take(NT), take(NT)]
        z_ga = take(NT)
        lev = [take(LW) for _ in range(3)]
        pooled = take(NT)
        nbias = take(SEQ)
        o_side = take(SEQ)
        attn = take(NT)
        th = take(NT)
        kv = take(3 * NB * P).rearrange("p (t x) -> p t x", t=3)
        q_bc = take(NB * P)
        rows = take(3 * P).rearrange("p (a x) -> p a x", a=3)
        pw_raw = take(512).rearrange("p (c d) -> p c d", c=2)
        st_nat = take(P)
        sc_s = take(48)
        ns_s = take(48)
        p_s = take(3 * P)
        pt_s = take(48)
        t16 = take(16)
        u_rows = take(2 * P).rearrange("p (a x) -> p a x", a=2)
        take = carver()
        mix_in = [take(NT) for _ in range(MIX_BUFS)]
        x_res = [take(SEQ + 2 * P) for _ in range(2)]
        y = take(QT * D_MODEL).rearrange("p (t d) -> p t d", t=QT)
        y_s = take(D_MODEL)
        y_t = [mix_in[0], mix_in[1]]
        ss_y = mix_in[2][:, 0:5 * KT].rearrange("p (t d) -> p t d", t=5)
        sq_junk = mix_in[3][:, 0:P]

        def wait_branch_split(eng, k):
            by_pool = k in POOL_SPLITS
            eng.wait_ge(m_split[by_pool], sum((i in POOL_SPLITS) == by_pool for i in range(k + 1)))

        def branch_tile(k):
            if k in RELOADED:
                return mix_in[RELOADED.index(k) % MIX_BUFS]
            return {6: z_gp[0], 7: z_gp[1], 15: attn}[k]

        ss, ms, sd, rstd = stat[:, 0:5], stat[:, 5:10], stat[:, 10:15], stat[:, 15:20]
        nmax, den, rden = stat[:, 20:24], stat[:, 24:28], stat[:, 28:32]
        nmax_s, den_s, rden_s = stat[0:16, 32:33], stat[0:16, 33:34], stat[0:16, 34:35]

        pj = [[bank(f"pj{a}{b}") for b in range(2)] for a in range(2)]
        ps_s = bank("ps_s")
        ps_t = bank("ps_t")
        ps_o = bank("ps_o")
        ps_m = bank("ps_m")
        banks = (pj[1][0], pj[1][1], ps_s, ps_t)

        x_in = [sem(f"x_in{i}") for i in range(QT)]
        xs_in, id_in = sem("xs_in"), sem("id_in")
        g_turned, g_ready, xg_done = sem("g_turned"), sem("g_ready"), sem("xg_done")
        sq_a, sq_p, sq_pm = sem("sq_a"), sem("sq_p"), sem("sq_pm")
        ss_done, rstd_st, rstd_in = sem("ss_done"), sem("rstd_st"), sem("rstd_in")
        g_in, tab_in, ps_in = sem("g_in"), sem("tab_in"), sem("ps_in")
        x_turned = sem("x_turned")
        x_hi_done = sem("x_hi_done")
        x_lo_done = sem("x_lo_done")
        ms_done, sd_done, rs_done = sem("ms_done"), sem("sd_done"), sem("rs_done")
        cleared = sem("cleared")
        raw_in = [sem(f"raw_in{i}") for i in range(SLOTS)]
        w_hi_done = sem("w_hi_done")
        w_lo_done = sem("w_lo_done")
        w_used = sem("w_used")
        tile_done = sem("tile_done")
        tile_out = sem("tile_out")
        qk_hi_done = sem("qk_hi_done")
        qk_split = sem("qk_split")
        qk_rows_t, qk_rows_c = sem("qk_rows_t"), sem("qk_rows_c")
        v_rows_t, v_rows_c = sem("v_rows_t"), sem("v_rows_c")
        k_nat_t, k_nat_c = sem("k_nat_t"), sem("k_nat_c")
        v_nat_t, v_nat_c = sem("v_nat_t"), sem("v_nat_c")
        v_hi_done, v_split = sem("v_hi_done"), sem("v_split")
        bias_done = sem("bias_done")
        scores = sem("scores")
        biased = sem("biased")
        exped = sem("exped")
        recip = sem("recip")
        normed = sem("normed")
        p_turned = sem("p_turned")
        pt_hi_done = sem("pt_hi_done")
        pt_split = sem("pt_split")
        pv_done = sem("pv_done")
        side_done = sem("side_done")
        o_done = sem("o_done")
        st_in, st_t, st_c = sem("st_in"), sem("st_t"), sem("st_c")
        lev_done = sem("lev_done")
        mean_done = sem("mean_done")
        pooled_hi_done, pooled_split = sem("pooled_hi_done"), sem("pooled_split")
        u_rows_t, u_rows_c = sem("u_rows_t"), sem("u_rows_c")
        pw_in, pw_hi_done, pw_split = sem("pw_in"), sem("pw_hi_done"), sem("pw_split")
        gp_tanh, gp_gate = sem("gp_tanh"), sem("gp_gate")
        ga_tanh, ga_gate = sem("ga_tanh"), sem("ga_gate")
        row_wr = sem("row_wr")
        vrow_wr = sem("vrow_wr")
        q_bc_in, kn_in, vn_in = sem("q_bc_in"), sem("kn_in"), sem("vn_in")
        k_in, v_in = sem("k_in"), sem("v_in")
        kq_prod, kq_done = sem("kq_prod"), sem("kq_done")
        kq_sum = sem("kq_sum")
        ns_done, ns_t, mx_s, ex_s, rc_s, nr_s, pt_s_t, pt_s_c = (
            sem("ns_done"), sem("ns_t"), sem("mx_s"), sem("ex_s"), sem("rc_s"), sem("nr_s"),
            sem("pt_s_t"), sem("pt_s_c"))
        pv_s = sem("pv_s")
        av_add = sem("av_add")
        av_hi_done, av_split = sem("av_hi_done"), sem("av_split")
        av_sum = sem("av_sum")
        pick = sem("pick")
        mixed = sem("mixed")
        mix_st, pmix_st = sem("mix_st"), sem("pmix_st")
        kn_st, vn_st, us_st, up_st = sem("kn_st"), sem("vn_st"), sem("us_st"), sem("up_st")
        kv_st, hist_st = sem("kv_st"), sem("hist_st")
        mix_back = [sem(f"mix_back{i}") for i in range(MIX_BUFS)]
        m_hi_done = sem("m_hi_done")
        m_split = (sem("m_split_v"), sem("m_split_p"))
        yt_done, y_turned, y_added, y_sq = sem("yt_done"), sem("y_turned"), sem("y_added"), sem("y_sq")
        xr_in = [sem("xr_in0"), sem("xr_in1")]
        y_scaled = sem("y_scaled")
        f_sum, f_ms, f_sd, f_rs, f_st = (
            sem("f_sum"), sem("f_ms"), sem("f_sd"), sem("f_rs"), sem("f_st"))
        f_out, f_out_a, f_out_s = sem("f_out"), sem("f_out_a"), sem("f_out_s")
        unit_starts, rows_seen, stores_seen = (
            sem("unit_starts"), sem("rows_seen"), sem("stores_seen"))
        IN_TILES = TPB * GROUPS
        IN_CHUNKS = NCH * PAIRS

        block = ctx.enter_context(nc.Block())

        @block.sync
        def _(sp):
            sp.dma_start(ident, consts[:, C_ID:C_ID + P]).then_inc(id_in, 16)
            sp.dma_start(g_rows[0:KT, :], norm_g[0].rearrange("(k p) -> k p", p=P)).then_inc(g_in, 16)
            sp.dma_start(x_smp[0:NB, :], xs).then_inc(xs_in, 16)
            for c in range(QT):
                cols = slice(SEQ * c, SEQ * c + SEQ)
                if c == QT - 1:
                    sp.dma_start(w_raw[:, 0, 0:CHUNKS[0][1], :],
                                 wi[:, 0:CHUNKS[0][1], COL_OF[0]:COL_OF[0] + P]).then_inc(raw_in[0], 16)
                sp.dma_start(x_nat[:, :, cols], xp[:, :, cols]).then_inc(x_in[c], 16)
            for c in (1, 2):
                lo, hi = CHUNKS[c]
                sp.dma_start(w_raw[:, c, 0:hi - lo, :],
                             wi[:, lo:hi, COL_OF[0]:COL_OF[0] + P]).then_inc(raw_in[c], 16)

            def load_chunk(n, slot, src):
                sp.wait_ge(w_lo_done, n - 2)
                lo, hi = CHUNKS[slot]
                sp.dma_start(w_raw[:, slot, 0:hi - lo, :], src).then_inc(raw_in[slot], 16)

            def load_out_chunk(d, c):
                n = IN_CHUNKS + 3 * d + c
                sp.wait_ge(w_lo_done, n - 2)
                cols = bass.ds(P * d, P)
                lo, hi = CHUNKS[c]
                sp.dma_start(w_raw[:, c, 0:hi - lo, :], wo[:, lo:hi, cols]).then_inc(raw_in[c], 16)

            def pair_loads(g, half, last=False):
                pr = 2 * g + half
                for j in range(NCH):
                    m = j + 3
                    lo, hi = CHUNKS[m % 3]
                    if m < NCH:
                        src = wi[:, lo:hi, bass.ds(COL_OF[m // 3] + P * pr, P)]
                    elif last:
                        load_out_chunk(0, m - NCH)
                        continue
                    else:
                        src = wi[:, lo:hi, bass.ds(COL_OF[0] + P * (pr + 1), P)]
                    load_chunk(NCH * pr + m, m % 3, src)
                    if j == 3:
                        sp.dma_start(st_nat[0:NB * HIST, :],
                                     st[:, bass.ds(P * pr, P)]).then_inc(st_in, 16)
                        for t, r in enumerate((128, 96, 96)):
                            sp.dma_start(kv[0:r, t, :].rearrange("p (b x) -> p b x", b=NB),
                                         k_rows[t][:, :, bass.ds(P * pr, P)]).then_inc(k_in, 16)
                        if half == 1:
                            sp.dma_start(pw_raw, pw[bass.ds(g, 1)].rearrange(
                                "a p c d -> (a p) c d")).then_inc(pw_in, 16)
                    if j == 11:
                        sp.wait_ge(k_nat_c, pr + 1)
                        sp.dma_start(k_out[:, :, bass.ds(P * pr, P)],
                                     k_nat.rearrange("p (t x) -> p t x", t=QT)).then_inc(kv_st, 16)
                    if j == 13:
                        sp.wait_ge(v_nat_c, pr + 1)
                        sp.dma_start(v_out[:, :, bass.ds(P * pr, P)],
                                     v_nat.rearrange("p (t x) -> p t x", t=QT)).then_inc(kv_st, 16)
                    if j == 14:
                        sp.wait_ge(kq_sum, 3 * pr + 3)
                        for t, r in enumerate((128, 96, 96)):
                            sp.dma_start(kv[0:r, t, :].rearrange("p (b x) -> p b x", b=NB),
                                         v_rows[t][:, :, bass.ds(P * pr, P)]).then_inc(v_in, 16)
                        sp.wait_ge(kv_st, 32 * pr + 32)
                        sp.sem_inc(stores_seen, 1)

            with sp.Fori(0, GROUPS - 1) as g:
                for half in range(2):
                    pair_loads(g, half)
            pair_loads(GROUPS - 1, 0)
            pair_loads(GROUPS - 1, 1, last=True)

            sp.wait_ge(v_rows_t, PAIRS)
            sp.wait_ge(qk_split, 2 * PAIRS)
            sp.wait_ge(v_split, PAIRS)
            sp.wait_ge(p_turned, 6 * PAIRS)
            for i, k in enumerate(RELOADED):
                if k < PAIRS:
                    sp.wait_ge(pmix_st, 16 * (k // 2 * 2 + 2))
                else:
                    sp.wait_ge(mix_st, 16 * (k - PAIRS + 1))
                if i >= MIX_BUFS:
                    wait_branch_split(sp, RELOADED[i - MIX_BUFS])
                sp.dma_start(mix_in[i % MIX_BUFS], mix_dram[k]).then_inc(mix_back[i % MIX_BUFS], 16)
                if i == MIX_BUFS - 1:
                    load_out_chunk(1, 0)
                    load_out_chunk(1, 1)
            load_out_chunk(1, 2)

            def load_res(d, q):
                sp.dma_start(x_res[q][:, 0:SEQ].rearrange("p (t x) -> p t x", t=QT),
                             xp[:, :, bass.ds(P * d, P)]).then_inc(xr_in[q], 16)
                sp.dma_start(x_res[q][0:NB, SEQ:SEQ + P],
                             xs[:, bass.ds(P * d, P)]).then_inc(xr_in[q], 16)
                sp.dma_start(x_res[q][:, SEQ + P:SEQ + 2 * P],
                             final_g[bass.ds(P * d, P)].partition_broadcast(P)).then_inc(xr_in[q], 16)
            wait_branch_split(sp, POOL_SPLITS[-1])
            wait_branch_split(sp, KT - 1)
            load_res(0, 0)
            load_res(1, 1)
            with sp.Fori(0, KT // 2 - 1) as i:
                for q in range(2):
                    for c in range(3):
                        load_out_chunk(2 * i + q + 2, c)
                    sp.wait_ge(y_scaled, 2 * i + q + 1)
                    load_res(2 * i + q + 2, q)
            for t in range(QT):
                if t < 2:
                    sp.wait_ge(f_out, t + 1)
                else:
                    sp.wait_ge(f_out_a, t - 1)
                sp.dma_start(yp[:, t, :], y[:, t, :]).then_inc(f_st, 16)
            sp.wait_ge(f_out_s, 1)
            sp.dma_start(ys_out, y_s[0:NB, :]).then_inc(f_st, 16)
            sp.wait_ge(f_st, 16 * (QT + 1))
            for s, n in ((kv_st, 2 * PAIRS), (kn_st, PAIRS), (vn_st, PAIRS),
                         (us_st, PAIRS), (up_st, PAIRS), (hist_st, 1), (mix_st, PAIRS - 1),
                         (pmix_st, PAIRS - 2), (row_wr, PAIRS), (vrow_wr, PAIRS)):
                sp.wait_ge(s, 16 * n)

        @block.tensor
        def _(pe):
            pe.wait_ge(id_in, 16)
            pe.wait_ge(g_in, 16)
            pe.transpose(ps_m[:, 0:KT], g_rows[0:KT, :], ident[0:KT, 0:KT]).then_inc(g_turned, 1)
            pe.wait_ge(xs_in, 16)
            for k in range(KT):
                tr = pe.transpose(ps_o[:, NB * k:NB * k + NB], x_smp[0:NB, P * k:P * k + P],
                                  ident[0:NB, 0:NB])
            tr.then_inc(g_turned, 1)
            for k in range(KT):
                pe.wait_ge(x_in[k // 4], 16)
                if k >= 4:
                    pe.wait_ge(x_lo_done, k - 2)
                for t in range(QT):
                    tr = pe.transpose(banks[k % 4][:, P * t:P * t + P],
                                      x_nat[:, t, P * k:P * k + P], ident)
                tr.then_inc(x_turned, 1)
            pe.sem_inc(w_used, 1)

            def chunk(n, slot, a, moving_split=False):
                pe.wait_ge(w_lo_done, n + 1)
                lo, hi = CHUNKS[slot]
                for k in range(lo, hi):
                    if moving_split:
                        wait_branch_split(pe, k)
                    whi, wlo = w_hi[:, slot, k - lo, :], w_lo[:, slot, k - lo, :]
                    for i, (w, m) in enumerate(((whi, mov_hi), (whi, mov_lo), (wlo, mov_hi))):
                        for h in range(2):
                            mm = pe.matmul(pj[a][h][:, 0:HT], w, m[:, k, HT * h:HT * h + HT],
                                           start=(k == 0 and i == 0), stop=(k == KT - 1 and i == 2))
                mm.then_inc(w_used, 1)

            def turn(dst, src, n=P):
                return pe.transpose(dst, src, ident[0:n, 0:n])

            def score(pr, h, u):
                pe.wait_ge(qk_split, 2 * pr + h + 1)
                if u > 0 or h > 0:
                    pe.wait_ge(biased, 8 * pr + 4 * h + (0, 2, 3)[u])
                for i, at in UNITS[u]:
                    n = P * (i + 1)
                    pe.matmul(ps_s[:, at:at + n], q_hl[:, P * i:P * i + P], k_hh[:, 0:n],
                              start=True, stop=False)
                    mm = pe.matmul(ps_s[:, at:at + n], q_hl[:, P * i:P * i + P], k_ll[:, 0:n],
                                   start=False, stop=True)
                mm.then_inc(scores, 1)

            def turn_p(pr, h, u):
                r = 3 * h + u
                pe.wait_ge(normed, 6 * pr + r + 1)
                if r > 0:
                    pe.wait_ge(pt_split, 6 * pr + r)
                for i, at in UNITS[u]:
                    for b in range(i + 1):
                        tr = turn(ps_t[:, at + P * b:at + P * b + P],
                                  pbuf[r % 2][:, at + P * b:at + P * b + P])
                tr.then_inc(p_turned, 1)

            def pv(pr, h):
                pe.wait_ge(pt_split, 6 * pr + 3 * h + 3)
                pe.wait_ge(v_split, pr + 1)
                if h == 1:
                    pe.wait_ge(o_done, 2 * pr + 1)
                for j in range(QT):
                    v = v_hl[:, j, 2 * E * h:2 * E * h + 2 * E]
                    pe.matmul(ps_o[:, P * j:SEQ], v, pt_hi[:, j, P * j:SEQ], start=(j == 0),
                              stop=False)
                    mm = pe.matmul(ps_o[:, P * j:SEQ], v, pt_lo[:, j, P * j:SEQ], start=False,
                                   stop=(j == QT - 1))
                mm.then_inc(pv_done, 1)

            with pe.Fori(0, GROUPS) as g:
                for half in range(2):
                    pr = 2 * g + half
                    for j in range(NCH):
                        tile = TPB * g + 6 * half + j // 3
                        if j % 3 == 0:
                            pe.wait_ge(tile_out, tile + 1)
                        if j < 3:
                            pe.wait_ge(x_lo_done, CHUNKS[j][1] + 1)
                        chunk(NCH * pr + j, j % 3, (j // 3) % 2)
                        if j == 6:
                            pe.wait_ge(tile_out, TPB * g + 6 * half + 4)
                            turn(ps_m[0:NB, 0:P], z_q[:, SEQ:NT])
                            turn(ps_m[0:NB, P:2 * P], z_k[:, SEQ:NT]).then_inc(qk_rows_t, 1)
                        if j in (7, 8, 9):
                            score(pr, 0, j - 7)
                        if j == 7:
                            pe.wait_ge(qk_rows_c, pr + 1)
                            for t in range(QT):
                                tr = turn(ps_m[:, P * t:P * t + P], z_k[:, P * t:P * t + P])
                            tr.then_inc(k_nat_t, 1)
                        if j == 9:
                            pe.wait_ge(k_nat_c, pr + 1)
                            pe.wait_ge(tile_out, TPB * g + 6 * half + 5)
                            for t in range(QT):
                                tr = turn(ps_m[:, P * t:P * t + P], z_v[:, P * t:P * t + P])
                            tr.then_inc(v_nat_t, 1)
                        if j in (9, 10, 11):
                            turn_p(pr, 0, j - 9)
                        if j == 10:
                            pe.wait_ge(v_nat_c, pr + 1)
                            turn(ps_m[0:NB, 0:P], z_v[:, SEQ:NT]).then_inc(v_rows_t, 1)
                        if j == 11:
                            pe.wait_ge(v_rows_c, pr + 1)
                            pe.wait_ge(st_in, 16 * pr + 16)
                            n = NB * HIST
                            turn(ps_m[:, 0:n], st_nat[0:n, :], n).then_inc(st_t, 1)
                        if j in (11, 12, 13):
                            score(pr, 1, j - 11)
                        if j == 12:
                            pv(pr, 0)
                            pe.wait_ge(st_c, pr + 1)
                            pe.wait_ge(ns_done, pr + 1)
                            for t in range(3):
                                tr = turn(ps_m[0:16, P * t:P * t + P], ns_s[:, 16 * t:16 * t + 16])
                            tr.then_inc(ns_t, 1)
                        if j == 13:
                            pe.wait_ge(id_in, 16)
                            pe.wait_ge(nr_s, pr + 1)
                            for t in range(3):
                                tr = turn(ps_m[:, 16 * t:16 * t + 16], p_s[0:16, P * t:P * t + P], 16)
                            tr.then_inc(pt_s_t, 1)
                        if j in (13, 14, 15):
                            turn_p(pr, 1, j - 13)
                        if j == 14:
                            pe.wait_ge(pt_s_c, pr + 1)
                            turn(ps_m[0:HIST, 0:P], lev[0][:, 16 + SEQ - HIST:16 + SEQ])
                            turn(ps_m[0:NB, P:2 * P], lev[0][:, 31 + SEQ:LW:16]).then_inc(u_rows_t, 1)
                        if j == 16:
                            pv(pr, 1)
                        if j == 17:
                            pe.wait_ge(u_rows_c, pr + 1)
                            pe.wait_ge(av_split, pr + 1)
                            for b, dst in ((0, ps_m), (1, ps_s)):
                                cols = slice(512 * b, 512 * b + 512)
                                pe.matmul(dst[:, :], ones_r[:, :], av_hi[:, cols], start=True,
                                          stop=False)
                                pe.matmul(dst[:, :], ones_r[:, :], av_lo[:, cols], start=False,
                                          stop=True).then_inc(av_sum, 1)
                for dt in range(2):
                    tile = TPB * g + 12 + dt
                    pe.wait_ge(tile_out, tile + 1)
                    pe.wait_ge(pw_split, g + 1)
                    pe.wait_ge(pooled_split, 2 * g + 2)
                    for ct in range(2):
                        whi = pw_hi[:, ct, P * dt:P * dt + P]
                        wlo = pw_lo[:, ct, P * dt:P * dt + P]
                        for i, (w, m) in enumerate(((whi, pooled_hi), (whi, pooled_lo),
                                                    (wlo, pooled_hi))):
                            for h in range(2):
                                mm = pe.matmul(pj[dt][h][:, 0:HT], w, m[:, ct, HT * h:HT * h + HT],
                                               start=(ct == 0 and i == 0), stop=(ct == 1 and i == 2))
                    mm.then_inc(tile_done, 1)

            def turn_y(d, q):
                pe.wait_ge(yt_done, d + 1)
                if not (isinstance(d, int) and d == 0):
                    pe.wait_ge(y_added, d)
                for t in range(QT):
                    turn(ps_t[:, P * t:P * t + P], y_t[q][:, P * t:P * t + P])
                turn(ps_m[0:NB, 0:P], y_t[q][:, SEQ:NT]).then_inc(y_turned, 1)

            for d in range(2):
                pe.wait_ge(tile_out, IN_TILES + d + 1)
                for c in range(3):
                    chunk(IN_CHUNKS + 3 * d + c, c, d, moving_split=(d == 0))
                    if d == 1 and c == 0:
                        turn_y(0, 0)
            with pe.Fori(0, KT // 2 - 1) as i:
                for q in range(2):
                    d = 2 * i + q + 2
                    pe.wait_ge(yt_done, d - 1)
                    for c in range(3):
                        chunk(IN_CHUNKS + 3 * d + c, c, q)
                        if c == 0:
                            turn_y(d - 1, 1 - q)
            turn_y(KT - 1, 1)

        @block.scalar
        def _(act):
            def split_hi(n, slot, count):
                lo, hi = CHUNKS[slot]
                act.wait_ge(raw_in[slot], 16 * count)
                if not (isinstance(n, int) and n < 3):
                    act.wait_ge(w_used, n - 1)
                act.activation(w_hi[:, slot, 0:hi - lo, :], w_raw[:, slot, 0:hi - lo, :],
                               ACT.Copy).then_inc(w_hi_done, 1)

            act.wait_ge(cleared, 1)
            act.activation(stat[:, 36:37], stat[:, 35:36], ACT.Sqrt)
            act.wait_ge(xs_in, 16)
            act.activation(junk_p[0:NB, :], x_smp[0:NB, :], ACT.Square,
                           accum_out=ss_x[0:NB, QT, 0:1]).then_inc(sq_p, 1)
            act.wait_ge(g_ready, 1)
            act.wait_ge(xg_done, 1)
            act.activation(mov_hi[:, :, SEQ:NT], xg_smp.rearrange("p (k b) -> p k b", k=KT),
                           ACT.Copy).then_inc(x_hi_done, 1)
            for k in range(KT):
                act.wait_ge(x_turned, k + 1)
                act.activation(mov_hi[:, k, 0:SEQ], banks[k % 4][:, :], ACT.Copy,
                               scale=g_t[:, k:k + 1]).then_inc(x_hi_done, 1)
                if k % 4 == 3:
                    c = k // 4
                    if c >= 2:
                        act.wait_ge(sq_a, c - 1)
                    act.activation(junk_a[c % 2], x_nat[:, 0, SEQ * c:SEQ * c + SEQ], ACT.Square,
                                   accum_out=ss_x[:, 0, c:c + 1]).then_inc(sq_a, 1)
                if k == 11:
                    split_hi(0, 0, 1)
            split_hi(1, 1, 1)
            split_hi(2, 2, 1)
            for t in (1, 2):
                act.activation(junk_l[t - 1], x_nat[:, t, :], ACT.Square,
                               accum_out=ss_x[:, t, 0:1]).then_inc(sq_a, 1)
            act.wait_ge(ms_done, 1)
            act.activation(sd, ms, ACT.Sqrt).then_inc(sd_done, 1)

            def qk_hi(pr, h):
                own, other = slice(E * h, E * h + E), slice(E * (1 - h), E * (1 - h) + E)
                if h == 1:
                    act.wait_ge(scores, 6 * pr + 3)
                act.activation(q_hl[own, :], z_q[own, 0:SEQ], ACT.Copy)
                act.activation(k_hh[own, :], z_k[own, 0:SEQ], ACT.Copy)
                act.activation(k_hh[other, :], z_k[own, 0:SEQ], ACT.Copy).then_inc(qk_hi_done, 1)

            def exps(pr, h, u):
                for i, at in UNITS[u]:
                    act.wait_ge(biased, 8 * pr + 4 * h + i + 1)
                    n = P * (i + 1)
                    pb_ = pbuf[(3 * h + u) % 2][:, at:at + n]
                    act.activation(pb_, pb_, ACT.Exp, scale=-1.0, bias=nmax[:, i:i + 1],
                                   accum_out=den[:, i:i + 1]).then_inc(exped, 1)

            def p_hi(pr, h, u):
                act.wait_ge(p_turned, 6 * pr + 3 * h + u + 1)
                if u == 0 and h == 1:
                    act.wait_ge(pv_done, 2 * pr + 1)
                for i, at in UNITS[u]:
                    a = act.activation(pt_hi[:, 0:i + 1, P * i:P * i + P],
                                       ps_t[:, at:at + P * (i + 1)].rearrange(
                                           "p (j x) -> p j x", j=i + 1), ACT.Copy)
                a.then_inc(pt_hi_done, 1)

            def side(pr, h):
                own, other = slice(E * h, E * h + E), slice(E * (1 - h), E * (1 - h) + E)
                act.wait_ge(pv_done, 2 * pr + h + 1)
                act.activation(o_side[own, :], ps_o[other, :], ACT.Copy).then_inc(side_done, 1)

            with act.Fori(0, GROUPS) as g:
                for half in range(2):
                    pr = 2 * g + half
                    for j in range(NCH):
                        n = j + 2
                        if j == 13:
                            act.wait_ge(mx_s, pr + 1)
                            act.activation(p_s[0:16, :], ps_m[0:16, 0:3 * P], ACT.Exp, scale=-1.0,
                                           bias=nmax_s, accum_out=den_s).then_inc(ex_s, 1)
                            side(pr, 0)
                        if j == 17:
                            act.wait_ge(av_add, 2 * pr + 2)
                            act.activation(av_hi[:, :], kv[:, 0, :], ACT.Copy).then_inc(av_hi_done, 1)
                        if j in (10, 11, 12):
                            p_hi(pr, 0, j - 10)
                        if j in (14, 15, 16):
                            p_hi(pr, 1, j - 14)
                        if j == 10:
                            act.wait_ge(v_nat_t, pr + 1)
                            act.activation(v_nat, ps_m[:, :], ACT.Copy).then_inc(v_nat_c, 1)
                            qk_hi(pr, 1)
                        if j > 0:
                            split_hi(NCH * pr + n, n % 3, 6 * pr + n // 3 + 1)
                        if j == 6:
                            act.wait_ge(tile_out, TPB * g + 6 * half + 4)
                            qk_hi(pr, 0)
                        if half == 1 and j == 7:
                            act.wait_ge(pw_in, 16 * g + 16)
                            act.activation(pw_hi[:, :, :], pw_raw, ACT.Copy).then_inc(pw_hi_done, 1)
                        if j == 8:
                            act.wait_ge(k_nat_t, pr + 1)
                            act.activation(k_nat, ps_m[:, :], ACT.Copy).then_inc(k_nat_c, 1)
                        if j in (8, 9, 10):
                            exps(pr, 0, j - 8)
                        if j == 11:
                            act.wait_ge(v_nat_c, pr + 1)
                            for h, at in ((0, 0), (1, 3 * E)):
                                a = act.activation(
                                    v_hl[:, :, at:at + E],
                                    v_nat.rearrange("p (t h e) -> p t h e", t=QT, h=2)[:, :, h],
                                    ACT.Copy)
                            a.then_inc(v_hi_done, 1)
                        if j in (12, 13, 14):
                            exps(pr, 1, j - 12)
                        if j == 15:
                            act.wait_ge(tile_out, TPB * g + 6 * half + 7)
                            act.activation(th, z_gp[half], ACT.Tanh).then_inc(gp_tanh, 1)
                        if j == 17:
                            act.wait_ge(mean_done, 3 * pr + 3)
                            act.activation(pooled_hi[:, half, :], pooled,
                                           ACT.Copy).then_inc(pooled_hi_done, 1)
                            side(pr, 1)
                    split_hi(NCH * pr + NCH + 2, 2, 6 * pr + 7)
                    act.wait_ge(tile_out, TPB * g + 6 * half + 8)
                    act.wait_ge(gp_gate, pr + 1)
                    act.activation(th, z_ga, ACT.Tanh).then_inc(ga_tanh, 1)

            for k in range(KT):
                if k in (0, CHUNKS[0][1], CHUNKS[1][1]):
                    act.wait_ge(w_used, IN_CHUNKS - 1 + (0, CHUNKS[0][1], CHUNKS[1][1]).index(k))
                if k in RELOADED:
                    i = RELOADED.index(k)
                    act.wait_ge(mix_back[i % MIX_BUFS], 16 * (i // MIX_BUFS + 1))
                elif k == 15:
                    act.wait_ge(mixed, PAIRS)
                else:
                    act.wait_ge(tile_out, IN_TILES + k - 5)
                act.activation(mov_hi[:, k, :], branch_tile(k), ACT.Copy).then_inc(m_hi_done, 1)
                if k == 12:
                    split_hi(IN_CHUNKS + 3, 0, 6 * PAIRS + 2)
            act.activation(stat[:, 36:37], stat[:, 35:36], ACT.Sqrt)

            def y_out(d, q):
                act.wait_ge(w_used, IN_CHUNKS + 3 * d + 4)
                if not (isinstance(d, int) and d < 2):
                    act.wait_ge(y_turned, d - 1)
                act.activation(y_t[q][:, 0:HT], pj[q][0][:, 0:HT], ACT.Copy)
                act.activation(y_t[q][:, HT:NT], pj[q][1][:, 0:HT], ACT.Copy).then_inc(yt_done, 1)

            def y_square(d):
                act.wait_ge(y_added, d + 1)
                for t in range(QT + 1):
                    n = P if t < QT else NB
                    src = y[:, t, bass.ds(P * d, P)] if t < QT else y_s[0:NB, bass.ds(P * d, P)]
                    if not (isinstance(d, int) and d == 0 and t == 0):
                        act.wait_ge(y_sq, 5 * d + t)
                    act.activation(sq_junk[0:n, :], src, ACT.Square,
                                   accum_out=ss_y[0:n, t, bass.ds(d, 1)]).then_inc(y_sq, 1)

            def out_pos(d, q, chunks=3):
                if not (isinstance(d, int) and d == 0):
                    y_out(d - 1, 1 - q)
                for c in range(chunks):
                    if not (isinstance(d, int) and d == 0 and c < 2):
                        n = 3 * d + c + 2
                        split_hi(IN_CHUNKS + n, (c + 2) % 3, 6 * PAIRS + d + (c + 2) // 3 + 1)
                if not (isinstance(d, int) and d == 0):
                    y_square(d - 1)

            out_pos(0, 0)
            out_pos(1, 1)
            with act.Fori(0, KT // 2 - 2) as i:
                for q in range(2):
                    out_pos(2 * i + q + 2, q)
            out_pos(KT - 2, 0)
            out_pos(KT - 1, 1, chunks=1)
            y_out(KT - 1, 1)
            y_square(KT - 1)
            act.wait_ge(f_ms, 1)
            act.activation(sd, ms, ACT.Sqrt).then_inc(f_sd, 1)
            act.wait_ge(f_rs, 4)
            act.wait_ge(y_scaled, KT)
            for t in (2, 3):
                act.activation(y[:, t, :], y[:, t, :], ACT.Copy,
                               scale=rstd[:, t:t + 1]).then_inc(f_out_a, 1)

        @block.gpsimd
        def _(pool):
            for c in range(QT):
                pool.wait_ge(x_in[c], 16)
                cols = slice(SEQ * c, SEQ * c + SEQ)
                if c == 0:
                    pool.wait_ge(sq_p, 1)
                pool.tensor_tensor(junk_p[:, cols], x_nat[:, 3, cols], x_nat[:, 3, cols],
                                   ALU.mult).then_inc(sq_pm, 1)
            pool.dma_start(tab[:, P:C_END], consts[:, P:C_END]).then_inc(tab_in, 16)
            with nc.allow_non_contiguous_dma(reason="1024 scales and 520 roots, once"):
                pool.dma_start(pscale[:, :], pool_scale[0].rearrange("(i p) -> p i", p=P)
                               ).then_inc(ps_in, 16)
                pool.wait_ge(rs_done, 4)
                pool.dma_start(rstd_dram[0:SEQ].rearrange("(t p) -> p t", p=P),
                               rstd[:, 0:QT]).then_inc(rstd_st, 16)
                pool.dma_start(rstd_dram[SEQ:NT].rearrange("(b x) -> b x", x=1),
                               rstd[0:NB, QT:QT + 1]).then_inc(rstd_st, 16)
            pool.wait_ge(rstd_st, 32)
            pool.dma_start(rstd_bc[:, :], rstd_dram.partition_broadcast(P)).then_inc(rstd_in, 16)
            pool.dma_start(pss_out[:, 0:HIST - 1, :], pss_in[:, 1:HIST, :]).then_inc(hist_st, 16)
            def group(g, last=False):
                for half in range(2):
                    pr = 2 * g + half
                    cols = bass.ds(P * pr, P)
                    pool.wait_ge(qk_rows_c, pr + 1)
                    pool.sem_inc(rows_seen, 1)
                    pool.dma_start(row_dram[0:2].rearrange("a b x -> b a x"),
                                   rows[0:NB, 0:2, :]).then_inc(row_wr, 16)
                    pool.dma_start(kn_out[:, cols], rows[0:NB, 1, :]).then_inc(kn_st, 16)
                    pool.wait_ge(row_wr, 16 * pr + 16)
                    pool.sem_inc(rows_seen, 1)
                    pool.dma_start(q_bc, row_dram[0].rearrange("b x -> (b x)").partition_broadcast(P)
                                   ).then_inc(q_bc_in, 16)
                    pool.dma_start(kv[96:97, 1, :], row_dram[1:2].rearrange("a b x -> a (b x)")
                                   ).then_inc(kn_in, 16)
                    pool.wait_ge(k_in, 48 * pr + 48)
                    pool.wait_ge(q_bc_in, 16 * pr + 16)
                    pool.wait_ge(kn_in, 16 * pr + 16)
                    for t, r in enumerate(ROWS_T):
                        pool.tensor_tensor(kv[0:r, t, :], kv[0:r, t, :], q_bc[0:r, :],
                                           ALU.mult).then_inc(kq_prod, 1)
                        kt = kv[0:r, t, :].rearrange("p (x e) -> p x e", e=E)
                        pool.wait_ge(kq_prod, 3 * pr + t + 1)
                        pool.tensor_tensor(kt[:, :, 0:E // 2], kt[:, :, 0:E // 2],
                                           kt[:, :, E // 2:E], ALU.add).then_inc(kq_done, 1)
                    pool.wait_ge(v_rows_c, pr + 1)
                    pool.sem_inc(rows_seen, 1)
                    pool.dma_start(row_dram[2], rows[0:NB, 2, :]).then_inc(vrow_wr, 16)
                    pool.dma_start(vn_out[:, cols], rows[0:NB, 2, :]).then_inc(vn_st, 16)
                    pool.wait_ge(vrow_wr, 16 * pr + 16)
                    pool.wait_ge(kq_sum, 3 * pr + 3)
                    pool.sem_inc(rows_seen, 1)
                    pool.dma_start(kv[96:97, 1, :], row_dram[2:3].rearrange("a b x -> a (b x)")
                                   ).then_inc(vn_in, 16)
                    pool.wait_ge(kn_st, 16 * pr + 16)
                    pool.wait_ge(vn_st, 16 * pr + 16)
                    pool.wait_ge(v_in, 48 * pr + 48)
                    pool.wait_ge(vn_in, 16 * pr + 16)
                    pool.wait_ge(pt_s_c, pr + 1)
                    for t, r in enumerate(ROWS_T):
                        vt = kv[0:r, t, :].rearrange("p (bh e) -> p bh e", e=E)
                        pb_ = pt_s[0:r, 16 * t:16 * t + 16].unsqueeze(2).to_broadcast([r, 16, E])
                        pool.tensor_tensor(vt, vt, pb_, ALU.mult).then_inc(pv_s, 1)
                    pool.wait_ge(u_rows_c, pr + 1)
                    pool.dma_start(pss_out[:, HIST - 1, cols], u_rows[0:NB, 1, :]).then_inc(us_st, 16)
                    pool.dma_start(psp_out[:, cols], u_rows[0:HIST, 0, :]).then_inc(up_st, 16)
                    pool.wait_ge(us_st, 16 * pr + 16)
                    pool.wait_ge(up_st, 16 * pr + 16)
                    if last and half == 1:
                        for k in POOL_SPLITS:
                            pool.wait_ge(m_hi_done, k + 1)
                            pool.tensor_tensor(mov_lo[:, k, :], branch_tile(k),
                                               mov_hi[:, k, :].bitcast(F32),
                                               ALU.subtract).then_inc(m_split[1], 1)
                    pool.wait_ge(ga_gate, pr + 1)
                    pool.wait_ge(o_done, 2 * pr + 2)
                    pool.wait_ge(pick, 4 * pr + 4)
                    pool.tensor_tensor(attn, attn, z_ga, ALU.mult).then_inc(mixed, 1)
                    if not (last and half == 1):
                        pool.wait_ge(mixed, pr + 1)
                        pool.dma_start(mix_dram[bass.ds(pr + PAIRS, 1)].rearrange(
                            "a p x -> (a p) x"), attn).then_inc(mix_st, 16)
                        pool.wait_ge(mix_st, 16 * pr + 16)
                if not last:
                    for dt in range(2):
                        pool.wait_ge(tile_out, TPB * g + 15 + dt)
                        pool.dma_start(mix_dram[bass.ds(2 * g + dt, 1)].rearrange(
                            "a p x -> (a p) x"), z_gp[dt]).then_inc(pmix_st, 16)
                    pool.wait_ge(pmix_st, 32 * g + 32)

            with pool.Fori(0, GROUPS - 1) as g:
                group(g)
            group(GROUPS - 1, last=True)

        @block.vector
        def _(dve):
            def rstd_of(done):
                dve.reciprocal(rstd, sd).then_inc(done, 1)
                dve.wait_ge(done, 1)
                dve.scalar_tensor_tensor(out=sd, in0=rstd, scalar=-0.5, in1=rstd, op0=ALU.mult,
                                         op1=ALU.mult).then_inc(done, 1)
                dve.wait_ge(done, 2)
                dve.tensor_tensor(sd, sd, ms, ALU.mult).then_inc(done, 1)
                dve.wait_ge(done, 3)
                dve.scalar_tensor_tensor(out=rstd, in0=sd, scalar=1.5, in1=rstd, op0=ALU.add,
                                         op1=ALU.mult).then_inc(done, 1)
                dve.wait_ge(done, 4)

            def split_lo(n, slot):
                lo, hi = CHUNKS[slot]
                dve.wait_ge(w_hi_done, n + 1)
                dve.tensor_tensor(w_lo[:, slot, 0:hi - lo, :], w_raw[:, slot, 0:hi - lo, :],
                                  w_hi[:, slot, 0:hi - lo, :].bitcast(F32),
                                  ALU.subtract).then_inc(w_lo_done, 1)

            dve.memset(stat[:, :], 0.0)
            dve.memset(ones_r[:, :].bitcast(F32), 1.0).then_inc(tile_out, 2)
            dve.memset(ss_x, 0.0).then_inc(cleared, 1)
            dve.wait_ge(g_turned, 1)
            dve.tensor_copy(g_t, ps_m[:, 0:KT]).then_inc(g_ready, 1)
            dve.wait_ge(g_turned, 2)
            dve.wait_ge(g_ready, 1)
            xg = xg_smp.rearrange("p (k b) -> p k b", k=KT)
            dve.tensor_tensor(xg, ps_o[:, 0:NB * KT].rearrange("p (k b) -> p k b", k=KT),
                              g_t.unsqueeze(2).to_broadcast([P, KT, NB]), ALU.mult).then_inc(xg_done, 1)
            dve.wait_ge(x_hi_done, 1)
            dve.tensor_tensor(mov_lo[:, :, SEQ:NT], xg, mov_hi[:, :, SEQ:NT].bitcast(F32),
                              ALU.subtract).then_inc(x_lo_done, 1)
            for k in range(KT):
                dve.wait_ge(x_hi_done, k + 2)
                dve.scalar_tensor_tensor(out=mov_lo[:, k, 0:SEQ], in0=banks[k % 4][:, :],
                                         scalar=g_t[:, k:k + 1],
                                         in1=mov_hi[:, k, 0:SEQ].bitcast(F32), op0=ALU.mult,
                                         op1=ALU.subtract).then_inc(x_lo_done, 1)
                if k == 11:
                    split_lo(0, 0)
            split_lo(1, 1)
            split_lo(2, 2)
            dve.wait_ge(sq_pm, QT)
            dve.tensor_reduce(ss_x[:, 3, 0:1], junk_p, AX_X, ALU.add).then_inc(ss_done, 1)
            dve.wait_ge(sq_a, QT + 2)
            dve.wait_ge(ss_done, 1)
            dve.tensor_reduce(ss, ss_x, AX_X, ALU.add).then_inc(ss_done, 1)
            dve.wait_ge(ss_done, 2)
            dve.tensor_scalar(ms, ss, 1.0 / D_MODEL, EPS, ALU.mult, ALU.add).then_inc(ms_done, 1)
            for b in lev:
                dve.memset(b[:, 0:16], 0.0).then_inc(cleared, 1)
            dve.memset(sc_s, 0.0).then_inc(cleared, 1)
            dve.wait_ge(sd_done, 1)
            rstd_of(rs_done)
            dve.wait_ge(cleared, 5)

            def take_tile(n, a, dsts, scale=1.0):
                dve.wait_ge(w_used, n + 2)
                for i, (dst, h, c0, c1) in enumerate(dsts):
                    o = dve.scalar_tensor_tensor(out=dst, in0=pj[a][h][:, c0:c1], scalar=scale,
                                                 in1=rstd_bc[:, HT * h + c0:HT * h + c1],
                                                 op0=ALU.mult, op1=ALU.mult)
                o.then_inc(tile_out, 1)

            def whole(z):
                return [(z[:, 0:HT], 0, 0, HT), (z[:, HT:NT], 1, 0, HT)]

            def qk_lo(pr, h):
                own, other = slice(E * h, E * h + E), slice(E * (1 - h), E * (1 - h) + E)
                dve.wait_ge(qk_hi_done, 2 * pr + h + 1)
                dve.tensor_tensor(q_hl[other, :], z_q[own, 0:SEQ], q_hl[own, :].bitcast(F32),
                                  ALU.subtract)
                for dst in (own, other):
                    o = dve.tensor_tensor(k_ll[dst, :], z_k[own, 0:SEQ], k_hh[own, :].bitcast(F32),
                                          ALU.subtract)
                o.then_inc(qk_split, 1)

            def head_bias(pr, h):
                if h == 1:
                    dve.wait_ge(biased, 8 * pr + 4)
                dve.scalar_tensor_tensor(out=nbias, in0=tab[:, C_DIST:C_DIST + SEQ],
                                         scalar=tab[:, bass.ds(2 * pr + h + C_SLOPE, 1)],
                                         in1=tab[:, C_NLOG:C_NLOG + SEQ], op0=ALU.mult,
                                         op1=ALU.add).then_inc(bias_done, 1)

            def bias_unit(pr, h, u):
                dve.wait_ge(scores, 6 * pr + 3 * h + u + 1)
                dve.wait_ge(bias_done, 2 * pr + h + 1)
                r = 3 * h + u
                if r >= 2:
                    dve.wait_ge(p_turned, 6 * pr + r - 1)
                dve.sem_inc(unit_starts, 1)
                for i, at in UNITS[u]:
                    n = P * (i + 1)
                    dve.tensor_tensor_reduce(out=pbuf[r % 2][:, at:at + n],
                                             in0=ps_s[:, at:at + n], in1=nbias[:, SEQ - n:SEQ],
                                             scale=1.0, scalar=3e38, op0=ALU.add, op1=ALU.min,
                                             accum_out=nmax[:, i:i + 1]).then_inc(biased, 1)

            def norm_unit(pr, h, u):
                for i, at in UNITS[u]:
                    n = P * (i + 1)
                    dve.wait_ge(exped, 8 * pr + 4 * h + i + 1)
                    dve.reciprocal(rden[:, i:i + 1], den[:, i:i + 1]).then_inc(recip, 1)
                    dve.wait_ge(recip, 8 * pr + 4 * h + i + 1)
                    pb_ = pbuf[(3 * h + u) % 2][:, at:at + n]
                    o = dve.tensor_scalar(pb_, pb_, rden[:, i:i + 1], None, ALU.mult)
                o.then_inc(normed, 1)

            def p_lo(pr, h, u):
                dve.wait_ge(pt_hi_done, 6 * pr + 3 * h + u + 1)
                for i, at in UNITS[u]:
                    blk = (slice(None), slice(0, i + 1), slice(P * i, P * i + P))
                    o = dve.tensor_tensor(pt_lo[blk],
                                          ps_t[:, at:at + P * (i + 1)].rearrange(
                                              "p (j x) -> p j x", j=i + 1),
                                          pt_hi[blk].bitcast(F32), ALU.subtract)
                o.then_inc(pt_split, 1)

            def head_out(pr, h):
                own = slice(E * h, E * h + E)
                dve.wait_ge(side_done, 2 * pr + h + 1)
                dve.tensor_tensor(attn[own, 0:SEQ], ps_o[own, :], o_side[own, :],
                                  ALU.add).then_inc(o_done, 1)

            def sum_keys(pr, t):
                r = ROWS_T[t]
                dve.wait_ge(kq_done, 3 * pr + t + 1)
                dve.tensor_reduce(sc_s[0:r, 16 * t:16 * t + 16],
                                  kv[0:r, t, :].rearrange("p (x e) -> p x e", e=E)[:, :, 0:E // 2],
                                  AX_X, ALU.add).then_inc(kq_sum, 1)

            def sample_bias(pr):
                dve.wait_ge(kq_sum, 3 * pr + 3)
                sbt = tab[:, C_SB:C_SB + 48].rearrange("p (t h) -> p t h", t=3)[
                    :, :, bass.ds(2 * pr, 2)].unsqueeze(2).to_broadcast([P, 3, NB, 2])
                dve.tensor_tensor(ns_s.rearrange("p (t b h) -> p t b h", t=3, b=NB),
                                  sc_s.rearrange("p (t b h) -> p t b h", t=3, b=NB),
                                  sbt, ALU.add).then_inc(ns_done, 1)

            samp = slice(31 + SEQ, LW, 16)
            def branch_lo(k):
                dve.wait_ge(m_hi_done, k + 1)
                dve.tensor_tensor(mov_lo[:, k, :], branch_tile(k), mov_hi[:, k, :].bitcast(F32),
                                  ALU.subtract).then_inc(m_split[0], 1)

            def group(g, last=False):
                for half in range(2):
                    pr = 2 * g + half
                    ch = NCH * pr
                    t0 = TPB * g + 6 * half
                    for j in range(NCH):
                        if j == 3:
                            dve.wait_ge(rstd_in, 16)
                            take_tile(ch + 2, 0, whole(z_q), -SCALE)
                        if j == 6:
                            take_tile(ch + 5, 1, whole(z_k))
                        if j == 9:
                            take_tile(ch + 8, 0, whole(z_v))
                        if j == 12:
                            take_tile(ch + 11, 1, [
                                (lev[0][:, 16:16 + HT], 0, 0, HT),
                                (lev[0][:, 16 + HT:16 + SEQ], 1, 0, SEQ - HT),
                                (lev[0][:, samp], 1, SEQ - HT, HT)])
                        if j == 15:
                            take_tile(ch + 14, 0, whole(z_gp[half]), 0.5)
                        if j == 13:
                            dve.wait_ge(ns_t, pr + 1)
                            dve.tensor_reduce(nmax_s, ps_m[0:16, 0:3 * P], AX_X,
                                              ALU.min).then_inc(mx_s, 1)
                        if j == 14:
                            dve.wait_ge(pt_s_t, pr + 1)
                            dve.tensor_copy(pt_s, ps_m[:, 0:48]).then_inc(pt_s_c, 1)
                        if j == 7:
                            dve.wait_ge(qk_rows_t, pr + 1)
                            dve.tensor_copy(rows[0:NB, 0:2, :], ps_m[0:NB, 0:2 * P].rearrange(
                                "p (a x) -> p a x", a=2)).then_inc(qk_rows_c, 1)
                            head_bias(pr, 0)
                        if j in (9, 10, 11):
                            norm_unit(pr, 0, j - 9)
                        if j in (13, 14, 15):
                            norm_unit(pr, 1, j - 13)
                        if j == 12:
                            dve.wait_ge(st_t, pr + 1)
                            dve.tensor_copy(
                                lev[0][:, 16 + SEQ:LW].rearrange("p (b s) -> p b s", b=NB)[:, :, 0:HIST],
                                ps_m[:, 0:NB * HIST].rearrange("p (b s) -> p b s", b=NB)
                            ).then_inc(st_c, 1)
                        if j in (8, 9, 10):
                            bias_unit(pr, 0, j - 8)
                        if j in (12, 13, 14):
                            bias_unit(pr, 1, j - 12)
                        if j in (10, 11, 12):
                            p_lo(pr, 0, j - 10)
                        if j in (14, 15, 16):
                            p_lo(pr, 1, j - 14)
                        if j == 11:
                            dve.wait_ge(v_rows_t, pr + 1)
                            dve.tensor_copy(rows[0:NB, 2, :], ps_m[0:NB, 0:P]).then_inc(v_rows_c, 1)
                        if j == 13:
                            dve.wait_ge(ex_s, pr + 1)
                            dve.reciprocal(rden_s, den_s).then_inc(rc_s, 1)
                            dve.wait_ge(rc_s, pr + 1)
                            dve.tensor_scalar(p_s[0:16, :], p_s[0:16, :], rden_s, None,
                                              ALU.mult).then_inc(nr_s, 1)
                        if j == 12:
                            sum_keys(pr, 2)
                            sample_bias(pr)
                        if j == 16:
                            dve.wait_ge(pv_s, 3 * pr + 3)
                            for t in (1, 2):
                                r = ROWS_T[t]
                                if t == 2:
                                    dve.wait_ge(av_add, 2 * pr + 1)
                                dve.tensor_tensor(kv[0:r, 0, :], kv[0:r, 0, :], kv[0:r, t, :],
                                                  ALU.add).then_inc(av_add, 1)
                        if j == 10:
                            qk_lo(pr, 1)
                        if j == 17:
                            dve.wait_ge(av_hi_done, pr + 1)
                            dve.tensor_tensor(av_lo[:, :], kv[:, 0, :], av_hi[:, :].bitcast(F32),
                                              ALU.subtract).then_inc(av_split, 1)
                        if j > 0:
                            split_lo(ch + j + 2, (j + 2) % 3)
                        if j == 6:
                            dve.wait_ge(tile_out, t0 + 4)
                            qk_lo(pr, 0)
                        if half == 1 and j == 8:
                            dve.wait_ge(pw_hi_done, g + 1)
                            dve.tensor_tensor(pw_lo[:, :, :], pw_raw, pw_hi[:, :, :].bitcast(F32),
                                              ALU.subtract).then_inc(pw_split, 1)
                        if j == 11:
                            dve.wait_ge(v_hi_done, pr + 1)
                            vn = v_nat.rearrange("p (t x) -> p t x", t=QT)
                            for h in range(2):
                                vh = v_hl[:, :, 3 * E * h:3 * E * h + E].bitcast(F32)
                                o = dve.tensor_tensor(v_hl[:, :, E * (1 + h):E * (2 + h)],
                                                      vn[:, :, E * h:E * h + E], vh, ALU.subtract)
                            o.then_inc(v_split, 1)
                            head_bias(pr, 1)
                            sum_keys(pr, 0)
                            sum_keys(pr, 1)
                        if j == 13:
                            head_out(pr, 0)
                        if j == 14:
                            dve.wait_ge(st_c, pr + 1)
                            dve.wait_ge(tile_out, t0 + 6)
                            dve.tensor_tensor(lev[1][:, 16:LW], lev[0][:, 16:LW],
                                              lev[0][:, 15:LW - 1], ALU.add).then_inc(lev_done, 1)
                        if j in (14, 15):
                            for i in ((0,) if j == 14 else (1, 2)):
                                s, src, dst = 2 << i, lev[1 + i % 2], lev[2 - i % 2]
                                dve.wait_ge(lev_done, 4 * pr + i + 1)
                                dve.scalar_tensor_tensor(
                                    out=dst[:, 16:LW], in0=src[:, 16 - s:LW - s],
                                    scalar=tab[:, bass.ds(3 * g + i + C_LM, 1)], in1=src[:, 16:LW],
                                    op0=ALU.mult, op1=ALU.add).then_inc(lev_done, 1)
                        if j == 15:
                            dve.wait_ge(u_rows_t, pr + 1)
                            dve.tensor_copy(u_rows[0:NB, 1, :], ps_m[0:NB, P:2 * P])
                            dve.tensor_copy(u_rows[0:HIST, 0, :], ps_m[0:HIST, 0:P]).then_inc(u_rows_c, 1)
                        if j == 16:
                            total, iw = lev[2], tab[:, bass.ds(g + C_IW, 1)]
                            dve.wait_ge(lev_done, 4 * pr + 4)
                            dve.tensor_tensor(t16, total[:, 16:32],
                                              tab[:, bass.ds(16 * g + C_INV, 16)],
                                              ALU.mult).then_inc(mean_done, 1)
                            dve.scalar_tensor_tensor(out=pooled[:, 16:SEQ], in0=total[:, 32:16 + SEQ],
                                                     scalar=iw, in1=lev[0][:, 32:16 + SEQ],
                                                     op0=ALU.mult, op1=ALU.subtract)
                            dve.scalar_tensor_tensor(out=pooled[:, SEQ:NT], in0=total[:, samp],
                                                     scalar=iw, in1=lev[0][:, samp], op0=ALU.mult,
                                                     op1=ALU.subtract).then_inc(mean_done, 1)
                            dve.wait_ge(mean_done, 3 * pr + 2)
                            dve.tensor_tensor(pooled[:, 0:16], t16, lev[0][:, 16:32],
                                              ALU.subtract).then_inc(mean_done, 1)
                        if j == 17:
                            dve.wait_ge(pooled_hi_done, pr + 1)
                            dve.tensor_tensor(pooled_lo[:, half, :], pooled,
                                              pooled_hi[:, half, :].bitcast(F32),
                                              ALU.subtract).then_inc(pooled_split, 1)
                            dve.wait_ge(gp_tanh, pr + 1)
                            dve.scalar_tensor_tensor(out=z_gp[half], in0=th, scalar=1.0,
                                                     in1=z_gp[half], op0=ALU.add,
                                                     op1=ALU.mult).then_inc(gp_gate, 1)
                    take_tile(ch + 17, 1, whole(z_ga), 0.5)
                    if half == 1:
                        dve.wait_ge(ps_in, 16)
                        for dt in range(2):
                            if last and dt == 1:
                                branch_lo(0)
                                branch_lo(1)
                            dve.wait_ge(tile_done, 2 * g + dt + 1)
                            for h in range(2):
                                c = slice(HT * h, HT * h + HT)
                                o = dve.scalar_tensor_tensor(
                                    out=z_gp[dt][:, c], in0=pj[dt][h][:, 0:HT],
                                    scalar=pscale[:, bass.ds(2 * g + dt, 1)], in1=z_gp[dt][:, c],
                                    op0=ALU.mult, op1=ALU.mult)
                            o.then_inc(tile_out, 1)
                    if last and half == 1:
                        for k in (2, 4, 6):
                            branch_lo(k)
                    split_lo(ch + NCH + 2, 2)
                    head_out(pr, 1)
                    dve.wait_ge(ga_tanh, pr + 1)
                    dve.scalar_tensor_tensor(out=z_ga, in0=th, scalar=1.0, in1=z_ga, op0=ALU.add,
                                             op1=ALU.mult).then_inc(ga_gate, 1)
                    for b, src in ((0, ps_m), (1, ps_s)):
                        dve.wait_ge(av_sum, 2 * pr + b + 1)
                        if b == 1:
                            dve.wait_ge(pick, 4 * pr + 2)
                        tmp = nbias.rearrange("p (b e) -> p b e", b=4)
                        dve.tensor_tensor(tmp, src[:, :].rearrange("p (b e) -> p b e", b=4),
                                          ident.unsqueeze(1).to_broadcast([P, 4, P]),
                                          ALU.mult).then_inc(pick, 1)
                        dve.wait_ge(pick, 4 * pr + 2 * b + 1)
                        dve.tensor_reduce(attn[:, SEQ + 4 * b:SEQ + 4 * b + 4], tmp, AX_X,
                                          ALU.add).then_inc(pick, 1)

            with dve.Fori(0, GROUPS - 1) as g:
                group(g)
            group(GROUPS - 1, last=True)

            for k in range(PAIRS, KT):
                if k not in POOL_SPLITS:
                    branch_lo(k)
                if k == 12:
                    split_lo(IN_CHUNKS + 3, 0)

            def add_res(d, q, count):
                dve.wait_ge(y_turned, d + 1)
                dve.wait_ge(xr_in[q], 48 * count + 48)
                dve.tensor_tensor(y[:, :, bass.ds(P * d, P)],
                                  ps_t[:, :].rearrange("p (t x) -> p t x", t=QT),
                                  x_res[q][:, 0:SEQ].rearrange("p (t x) -> p t x", t=QT), ALU.add)
                dve.tensor_tensor(y_s[0:NB, bass.ds(P * d, P)], ps_m[0:NB, 0:P],
                                  x_res[q][0:NB, SEQ:SEQ + P], ALU.add).then_inc(y_added, 1)

            def scale_y(d, q):
                dve.wait_ge(y_sq, 5 * d + 5)
                gf = x_res[q][:, SEQ + P:SEQ + 2 * P]
                ys, yss = y[:, :, bass.ds(P * d, P)], y_s[0:NB, bass.ds(P * d, P)]
                dve.tensor_tensor(ys, ys, gf.unsqueeze(1).to_broadcast([P, QT, P]), ALU.mult)
                dve.tensor_tensor(yss, yss, gf[0:NB, :], ALU.mult).then_inc(y_scaled, 1)

            def out_pos(d, q, count, chunks=3):
                first = isinstance(d, int) and d == 0
                for c in range(chunks):
                    if not (first and c < 2):
                        split_lo(IN_CHUNKS + 3 * d + c + 2, (c + 2) % 3)
                    if c == 1 and not first:
                        add_res(d - 1, 1 - q, count)
                if not first:
                    if chunks == 1:
                        add_res(d - 1, 1 - q, count)
                    scale_y(d - 1, 1 - q)

            wait_branch_split(dve, POOL_SPLITS[-1])
            wait_branch_split(dve, KT - 1)
            dve.memset(ss_y, 0.0).then_inc(cleared, 1)
            out_pos(0, 0, 0)
            out_pos(1, 1, 0)
            with dve.Fori(0, KT // 2 - 2) as i:
                for q in range(2):
                    out_pos(2 * i + q + 2, q, i + q)
            out_pos(KT - 2, 0, KT // 2 - 2)
            out_pos(KT - 1, 1, KT // 2 - 1, chunks=1)
            add_res(KT - 1, 1, KT // 2 - 1)
            dve.wait_ge(y_sq, 5 * KT)
            dve.tensor_reduce(ss, ss_y, AX_X, ALU.add).then_inc(f_sum, 1)
            dve.wait_ge(f_sum, 1)
            dve.tensor_scalar(ms, ss, 1.0 / D_MODEL, EPS, ALU.mult, ALU.add).then_inc(f_ms, 1)
            scale_y(KT - 1, 1)
            dve.wait_ge(y_scaled, KT)
            dve.wait_ge(f_sd, 1)
            rstd_of(f_rs)
            for t in range(2):
                dve.tensor_scalar(y[:, t, :], y[:, t, :], rstd[:, t:t + 1], None,
                                  ALU.mult).then_inc(f_out, 1)
            dve.tensor_scalar(y_s[0:NB, :], y_s[0:NB, :], rstd[0:NB, QT:QT + 1], None,
                              ALU.mult).then_inc(f_out_s, 1)

    return nc


INS = ("x_prompt", "x_sample", "state_pool", "cache_k_win", "cache_v_win", "norm_g", "w_in",
       "pool_w", "pool_scale", "w_out", "final_norm_g")
OUTS = ((1, SEQ, D_MODEL), (NB, 1, D_MODEL), (1, 1, HIST, D_HALF), (1, 1, SEQ, HEADS, E),
        (1, 1, SEQ, HEADS, E), (1, NB, HIST, D_HALF), (1, NB, 1, HEADS, E), (1, NB, 1, HEADS, E))


def kernel(**inputs):
    import concourse.bacc as bacc
    from concourse.bass_utils import run_bass_kernel_spmd

    nc = bacc.Bacc("TRN2", target_bir_lowering=False, num_devices=1)
    arrays, args = {}, []
    for name in INS:
        a = np.ascontiguousarray(inputs[name])
        arrays[f"in_{name}"] = a
        args.append(nc.dram_tensor(f"in_{name}", a.shape, mybir.dt.from_np(a.dtype),
                                   kind="ExternalInput").ap())
    arrays["in_tables"] = constants()
    args.append(nc.dram_tensor("in_tables", (P, C_END), F32, kind="ExternalInput").ap())
    for i, shape in enumerate(OUTS):
        args.append(nc.dram_tensor(f"out_{i}", shape, F32, kind="ExternalOutput").ap())
    layer_step(nc, *args)
    r = run_bass_kernel_spmd(nc, [arrays], core_ids=[0])
    return tuple(r.results[0][f"out_{i}"] for i in range(len(OUTS)))
```
